# Optimizing a Trainium2 kernel written in Bass

```python
import jax, jax.numpy as jnp
from jax import lax
import numpy as np

D_MODEL = 1024
BATCH = 1
SEQ = 512
DEPTH = 2

N_MIXERS = 3
N_A = len(range(0, DEPTH, N_MIXERS))
N_B = len(range(1, DEPTH, N_MIXERS))
N_C = len(range(2, DEPTH, N_MIXERS))
N_SUBLAYERS = 3
N_MOD = 3
CONV_WIDTH = 31
N_HEADS = 16
HEAD_DIM = D_MODEL // N_HEADS
Q_BLOCK = 128
POOL_WINDOWS = (2, 4, 8, 16)
POOL_GROUPS = len(POOL_WINDOWS)
POOL_GROUP_DIM = D_MODEL // POOL_GROUPS
D_FF = ((8 * D_MODEL // 3 + 127) // 128) * 128
EPS = 1e-6

kernel_name = "hybrid_conv_stickbreak_pool_macaron"

def _bc(v, ndim):
    return v.reshape((1,) * (ndim - v.ndim) + v.shape)

def rms_norm(x, g):
    xf = x.astype(jnp.float32)
    y = xf * lax.rsqrt(jnp.mean(xf * xf, axis=-1, keepdims=True) + EPS)
    return (y * _bc(g.astype(jnp.float32), x.ndim)).astype(x.dtype)

def layer_norm(x, g, b):
    xf = x.astype(jnp.float32)
    mu = jnp.mean(xf, axis=-1, keepdims=True)
    var = jnp.mean(jnp.square(xf - mu), axis=-1, keepdims=True)
    y = (xf - mu) * lax.rsqrt(var + EPS)
    y = y * _bc(g.astype(jnp.float32), x.ndim) + _bc(b.astype(jnp.float32), x.ndim)
    return y.astype(x.dtype)

def modulate(x, g, shift, scale):
    return rms_norm(x, g) * (1 + scale[:, None, :]) + shift[:, None, :]

def swiglu(h, w1, w3, w2):
    return (jax.nn.silu(h @ w1) * (h @ w3)) @ w2

def conformer_conv(h, w_in, b_in, dw, dw_b, ln_g, ln_b, w_out, b_out):
    u = jax.nn.glu(h @ w_in + _bc(b_in, 3), axis=-1)
    v = lax.conv_general_dilated(
        u, dw[:, None, :].astype(u.dtype), window_strides=(1,),
        padding=[(CONV_WIDTH - 1, 0)],
        dimension_numbers=("NWC", "WIO", "NWC"),
        feature_group_count=D_MODEL) + _bc(dw_b, 3)
    v = jax.nn.silu(layer_norm(v, ln_g, ln_b))
    return v @ w_out + _bc(b_out, 3)

def stick_breaking_attention(h, w_qkv, q_g, k_g, w_o):
    B, S, _ = h.shape
    qkv = h @ w_qkv
    q, k, v = jnp.split(qkv, 3, axis=-1)
    to_heads = lambda t: t.reshape(B, S, N_HEADS, HEAD_DIM).transpose(0, 2, 1, 3)
    q = rms_norm(to_heads(q), q_g)
    k = rms_norm(to_heads(k), k_g)
    qf = q.astype(jnp.float32) * (HEAD_DIM ** -0.5)
    kf = k.astype(jnp.float32)
    vf = to_heads(v).astype(jnp.float32)
    nb = S // Q_BLOCK
    q_blocks = qf.reshape(B, N_HEADS, nb, Q_BLOCK, HEAD_DIM).transpose(2, 0, 1, 3, 4)
    key_pos = jnp.arange(S)

    def block(args):
        qb, bi = args
        z = jnp.einsum('bhqd,bhkd->bhqk', qb, kf)
        t = bi * Q_BLOCK + jnp.arange(Q_BLOCK)
        mask = (key_pos[None, :] < t[:, None])[None, None]
        neg_log_keep = jnp.where(mask, jax.nn.softplus(z), 0.0)
        rcs = lax.cumsum(neg_log_keep, axis=3, reverse=True)
        suffix = jnp.concatenate([rcs[..., 1:], jnp.zeros_like(rcs[..., :1])], axis=-1)
        a = jnp.where(mask, jnp.exp(jax.nn.log_sigmoid(z) - suffix), 0.0)
        return jnp.einsum('bhqk,bhkd->bhqd', a, vf)

    o = lax.map(block, (q_blocks, jnp.arange(nb)))
    o = o.transpose(1, 0, 3, 2, 4).reshape(B, S, D_MODEL).astype(h.dtype)
    return o @ w_o

def multiscale_pool(h, p_w, p_b, p_scale):
    B, S, _ = h.shape
    hf = h.astype(jnp.float32)
    cs0 = jnp.concatenate([jnp.zeros((B, 1, D_MODEL), jnp.float32), lax.cumsum(hf, axis=1)], axis=1)
    t = jnp.arange(S)
    diffs = []
    for g, w in enumerate(POOL_WINDOWS):
        sl = slice(g * POOL_GROUP_DIM, (g + 1) * POOL_GROUP_DIM)
        c_g = cs0[:, :, sl]
        lag = jnp.concatenate([jnp.zeros((B, w - 1, POOL_GROUP_DIM), jnp.float32), c_g[:, :S + 1 - w]], axis=1)
        cnt = jnp.minimum(t + 1, w).astype(jnp.float32)[None, :, None]
        diffs.append((c_g[:, 1:] - lag) / cnt - hf[:, :, sl])
    d = jnp.stack(diffs, axis=2)
    y = jnp.einsum('bsgc,gcd->bsgd', d, p_w.astype(jnp.float32)) + _bc(p_b.astype(jnp.float32), 4)
    return (y.reshape(B, S, D_MODEL) * _bc(p_scale.astype(jnp.float32), 3)).astype(h.dtype)

def setup_inputs(seed: int = 0) -> dict:
    key = jax.random.key(seed)
    ks = jax.random.split(key, 26)
    n = lambda k, shape, s: jax.random.normal(k, shape, jnp.float32) * s
    D, F, G = D_MODEL, D_FF, POOL_GROUP_DIM
    return {
        "x": n(ks[0], (BATCH, SEQ, D), 1.0),
        "c": n(ks[1], (BATCH, D), 1.0),
        "cond_w": n(ks[2], (D, D), D ** -0.5),
        "cond_b": n(ks[3], (D,), 0.02),
        "ada_w": n(ks[4], (DEPTH, D, N_SUBLAYERS * N_MOD * D), 0.1 * D ** -0.5),
        "ada_b": n(ks[5], (DEPTH, N_SUBLAYERS * N_MOD * D), 0.02),
        "norm_g": 1.0 + n(ks[6], (DEPTH, N_SUBLAYERS, D), 0.02),
        "ffn_w1": n(ks[7], (DEPTH, 2, D, F), D ** -0.5),
        "ffn_w3": n(ks[8], (DEPTH, 2, D, F), D ** -0.5),
        "ffn_w2": n(ks[9], (DEPTH, 2, F, D), F ** -0.5),
        "a_w_in": n(ks[10], (N_A, D, 2 * D), D ** -0.5),
        "a_b_in": n(ks[11], (N_A, 2 * D), 0.02),
        "a_dw": n(ks[12], (N_A, CONV_WIDTH, D), CONV_WIDTH ** -0.5),
        "a_dw_b": n(ks[13], (N_A, D), 0.02),
        "a_ln_g": 1.0 + n(ks[14], (N_A, D), 0.02),
        "a_ln_b": n(ks[15], (N_A, D), 0.02),
        "a_w_out": n(ks[16], (N_A, D, D), D ** -0.5),
        "a_b_out": n(ks[17], (N_A, D), 0.02),
        "b_w_qkv": n(ks[18], (N_B, D, 3 * D), D ** -0.5),
        "b_q_g": 1.0 + n(ks[19], (N_B, HEAD_DIM), 0.02),
        "b_k_g": 1.0 + n(ks[20], (N_B, HEAD_DIM), 0.02),
        "b_w_o": n(ks[21], (N_B, D, D), D ** -0.5),
        "p_w": n(ks[22], (N_C, POOL_GROUPS, G, G), G ** -0.5),
        "p_b": n(ks[23], (N_C, POOL_GROUPS, G), 0.02),
        "p_scale": 1.0 + n(ks[24], (N_C, D), 0.1),
    }

def reference(x, c, cond_w, cond_b, ada_w, ada_b, norm_g, ffn_w1, ffn_w3, ffn_w2,
              a_w_in, a_b_in, a_dw, a_dw_b, a_ln_g, a_ln_b, a_w_out, a_b_out,
              b_w_qkv, b_q_g, b_k_g, b_w_o, p_w, p_b, p_scale):
    B = x.shape[0]
    e = jax.nn.silu(c @ cond_w + cond_b[None, :])
    ia = ib = ic = 0
    for i in range(DEPTH):
        mod = (e @ ada_w[i] + ada_b[i][None, :]).reshape(B, N_SUBLAYERS, N_MOD, D_MODEL)
        shift, scale, gate = mod[:, :, 0], mod[:, :, 1], 1 + mod[:, :, 2]
        h = modulate(x, norm_g[i, 0], shift[:, 0], scale[:, 0])
        x = x + 0.5 * gate[:, 0][:, None, :] * swiglu(h, ffn_w1[i, 0], ffn_w3[i, 0], ffn_w2[i, 0])
        h = modulate(x, norm_g[i, 1], shift[:, 1], scale[:, 1])
        kind = i % N_MIXERS
        if kind == 0:
            y = conformer_conv(h, a_w_in[ia], a_b_in[ia], a_dw[ia], a_dw_b[ia],
                               a_ln_g[ia], a_ln_b[ia], a_w_out[ia], a_b_out[ia])
            ia += 1
        elif kind == 1:
            y = stick_breaking_attention(h, b_w_qkv[ib], b_q_g[ib], b_k_g[ib], b_w_o[ib])
            ib += 1
        else:
            y = multiscale_pool(h, p_w[ic], p_b[ic], p_scale[ic])
            ic += 1
        x = x + gate[:, 1][:, None, :] * y
        h = modulate(x, norm_g[i, 2], shift[:, 2], scale[:, 2])
        x = x + 0.5 * gate[:, 2][:, None, :] * swiglu(h, ffn_w1[i, 1], ffn_w3[i, 1], ffn_w2[i, 1])
    return x


_drawn_inputs = setup_inputs


def setup_inputs(seed=0):
    import zlib

    import numpy as np

    out = dict(_drawn_inputs(seed))
    spreads = {}
    factors = {'cond_b': 8.0,
     'a_b_in': 4.394,
     'a_ln_g': 4.194,
     'a_ln_b': 4.71,
     'a_b_out': 2.816,
     'b_q_g': 8.0,
     'b_k_g': 22.63}
    for name, (base, spread) in spreads.items():
        noise = np.random.default_rng([zlib.crc32(name.encode()), seed]).standard_normal(out[name].shape)
        drawn = base * np.exp(spread * noise) if base else spread * noise
        out[name] = __import__('jax').numpy.asarray(drawn.astype(out[name].dtype))
    for name, factor in factors.items():
        out[name] = (out[name] * factor).astype(out[name].dtype)
    return out
```

```python
from contextlib import ExitStack

import numpy as np
import concourse.bass as bass
from concourse import mybir

F32 = mybir.dt.float32
F32R = mybir.dt.float32r
ALU = mybir.AluOpType
ACT = mybir.ActivationFunctionType

P = 128
S = 512
D = 1024
F = 2816
KD = D // P
KF = F // P
HF = KF // 2
W = 31
TP = 13
TV = W - TP
HEADS = 16
HD = D // HEADS
EPS = 1e-6
EXP_LN_SET = 6
NEG = -1.0e30
SLAB = KD * 2 * P
DOWN = HF * P
DIAG = TP * P
GW = 512
NFFN = 4
QL = S + (S - P) + P + (S - 2 * P)

N_UP = [0, 58, 96, 150]
N_DOWN = [n + KF for n in N_UP]
N_CONV = N_DOWN[0] + 2 * KD
N_OUT = N_CONV + 2 * KD
N_QKV = N_DOWN[2] + 2 * KD
N_WO = N_QKV + 12
assert N_UP[1] == N_OUT + 4 and N_UP[3] == N_WO + 4
CIN = [N_CONV] + [N_CONV + 2 * c - 1 for c in range(1, KD)]
CTAP = [N_CONV + 2 * c + 2 for c in range(KD - 1)] + [N_OUT - 1]
N_OF = [n for n in range(N_UP[3] + KF + 2 * KD) if n not in CTAP]
R_OF = {n: r for r, n in enumerate(N_OF)}

VEC = {}
_at = 0
for _name, _n in (("norm_g", 6 * KD), ("ada_b", 2 * 9 * KD), ("cond_b", KD), ("c", KD), ("b_in", 2 * KD),
                  ("dw_b", KD), ("ln_g", KD), ("ln_b", KD), ("b_out", KD), ("qk_g", 2)):
    VEC[_name] = _at
    _at += _n
NVEC = _at

Q_FFN = [6, 20, 31]
Q_BODIES = [11, 11, 7, 0]
Q_OUT = 17


def trunk(nc, x_in, up_in, down_in, mix_in, ada_in, vec_in, dw_in, con_in, ind_in, sel_in, out):
    ctx = ExitStack()
    with ctx:
        def sb(name, shape, dt=F32):
            return ctx.enter_context(nc.sbuf_tensor(name, shape, dt))

        def sem(name):
            return ctx.enter_context(nc.semaphore(name))

        x = sb("x", [P, KD, S])
        h_hi = sb("h_hi", [P, KD, S], F32R)
        h_lo = sb("h_lo", [P, KD, S], F32R)
        act_tmp = sb("act_tmp", [P, 2, S])
        sq_tmp = sb("sq_tmp", [P, 2, S])
        ss = sb("ss", [P, S])
        ada_acc = sb("ada_acc", [P, GW])
        ident = sb("ident", [P, P])
        ones = sb("ones", [P, P])
        vec = sb("vec", [P, NVEC])
        mods = sb("mods", [P, 2 * 9 * KD])
        e_pre = sb("e_pre", [P, KD])
        e_col = sb("e_col", [P, KD])
        gs = sb("gs", [P, KD])
        gt = sb("gt", [P, KD])
        st = sb("st", [P, 24])
        raw0 = sb("raw0", [P, SLAB])
        w0 = sb("w0", [P, 2, SLAB], F32R)
        raw = [raw0, None]
        wsp = [w0, None]

        with ExitStack() as scope:
            def ov(name, shape, dt=F32):
                return scope.enter_context(nc.sbuf_tensor(name, shape, dt))
            raw[1] = ov("raw1", [P, SLAB])
            wsp[1] = ov("w1", [P, 2, SLAB], F32R)
            ada_raw = ov("ada_raw", [P, 4, GW])
            g_hi = ov("g_hi", [P, KF, S], F32R)
            g_lo = ov("g_lo", [P, KF, S], F32R)
        with ExitStack() as scope:
            ov("pad_a", [P, 4 * SLAB])
            stage = [ov(f"stage{i}", [P, 4, GW]) for i in range(6)]
        with ExitStack() as scope:
            ov("pad_b", [P, 4 * SLAB])
            v = ov("v", [P, KD, S])
            u = ov("u", [P, 2, S + W - 1])
            u_hi = ov("u_hi", [P, 2, S + W - 1], F32R)
            u_lo = ov("u_lo", [P, 2, S + W - 1], F32R)
            v_odd = ov("v_odd", [P, S])
            v_sum = ov("v_sum", [P, S])
            diag = ov("diag", [P, DIAG])
            dw = ov("dw", [P, KD, W])
        with ExitStack() as scope:
            sp_abs = ov("sp_abs", [P, 2, QL])
            sp_hi = ov("sp_hi", [P, QL], F32R)
            sp_lo = ov("sp_lo", [P, QL], F32R)
            a_hi = ov("a_hi", [P, QL], F32R)
            a_lo = ov("a_lo", [P, QL], F32R)
            ov("pad_c", [P, S])
            qk = ov("qk", [P, 2 * KD, S])
            v_hi = ov("v_hi", [P, 4, D], F32R)
            v_lo = ov("v_lo", [P, 4, D], F32R)
            qk_s = ov("qk_s", [P, 2, 4, S], F32R)
            con = ov("con", [P, 4, P], F32R)
            a_f = ov("a_f", [P, QL])
        with ExitStack() as scope:
            ov("pad_d", [P, 3 * SLAB])
            sel = ov("sel", [32, KD, P], F32R)
            ov("pad_e", [P, KD * P])
            ov("pad_f", [P, 2 * KD * S + 2 * 4 * D])
            y = ov("y", [32, 4, S])
            y_hi = ov("y_hi", [32, S], F32R)
            y_lo = ov("y_lo", [32, S], F32R)
            sel_f = ov("sel_f", [32, KD, P])
            ov("pad_g", [P, 4 * P])
            con_f = ov("con_f", [P, 4, P])
            ind = ov("ind", [P, KD, 32])

        ps = ctx.enter_context(nc.psum_tensor("ps", [P, 8, S], F32))
        pair = [[ps[:, 0, :], ps[:, 1, :]], [ps[:, 2, :], ps[:, 3, :]]]
        down_ps = [ps[:, 4, :], ps[:, 5, :]]
        row = ps[:, 6, :]
        ada_ps = ps[:, 7, 0:4]
        zps = ps[:, :, :].rearrange("p b s -> p (b s)")

        x_in_s = [sem(f"x_in{i}") for i in range(2)]
        vec_s = sem("vec_in")
        stage_s = [sem(f"stage_in{i}") for i in range(6)]
        raw_s = [sem("raw0_in"), sem("raw1_in")]
        ada_s = sem("ada_in")
        dw_s = sem("dw_in")
        con_s = sem("con_in")
        out_s = sem("out_written")
        ones_done = sem("ones_done")
        hi_done = sem("hi_done")
        lo_done = sem("lo_done")
        slab_done = sem("slab_done")
        ada_step = sem("ada_step")
        ada_sum = sem("ada_sum")
        mod_done = sem("mod_done")
        e_done = sem("e_done")
        sq_done = sem("sq_done")
        ss_step = sem("ss_step")
        stat_done = sem("stat_done")
        vec_step = sem("vec_step")
        sqrt_done = sem("sqrt_done")
        fac_step = sem("fac_step")
        gs_done = sem("gs_done")
        gate_done = sem("gate_done")
        rdiag_done = sem("rdiag_done")
        row_done = sem("row_done")
        t_done = sem("t_done")
        hhi_done = sem("hhi_done")
        h_done = sem("h_done")
        silu_done = sem("silu_done")
        g_full = sem("g_full")
        ghi_done = sem("ghi_done")
        g_done = sem("g_done")
        x_done = sem("x_done")
        sig_done = sem("sig_done")
        u_done = sem("u_done")
        uhi_done = sem("uhi_done")
        ulo_done = sem("ulo_done")
        tap_step = sem("tap_step")
        vodd_done = sem("vodd_done")
        bo_step = sem("bo_step")
        v_done = sem("v_done")
        diag_done = sem("diag_done")
        pad_done = sem("pad_done")
        vsum_step = sem("vsum_step")
        mean_done = sem("mean_done")
        vc_done = sem("vc_done")
        yact_done = sem("yact_done")
        conr_done = sem("conr_done")
        qk_done = sem("qk_done")
        qksq_done = sem("qksq_done")
        ind_done = sem("ind_done")
        yv_done = sem("yv_done")
        ysq_done = sem("ysq_done")
        yn_step = sem("yn_step")
        y_done = sem("y_done")
        bc_done = sem("bc_done")
        qkn_done = sem("qkn_done")
        vhi_done = sem("vhi_done")
        vlo_done = sem("vlo_done")
        qks_step = sem("qks_step")
        z_done = sem("z_done")
        ln_step = sem("ln_step")
        sp_done = sem("sp_done")
        sphi_done = sem("sphi_done")
        splo_done = sem("splo_done")
        cum_done = sem("cum_done")
        a_done = sem("a_done")
        ahi_done = sem("ahi_done")
        alo_done = sem("alo_done")
        av_done = sem("av_done")
        ohi_done = sem("ohi_done")
        o_done = sem("o_done")

        block = ctx.enter_context(nc.Block())

        def vcol(name, i, n=1):
            return vec[:, VEC[name] + i:VEC[name] + i + n]

        def mod(layer, sub, which, i=0, n=KD):
            at = ((layer * 3 + sub) * 3 + which) * KD + i
            return mods[:, at:at + n]

        def f32(ap):
            return ap.bitcast(F32)

        def t_buf(c):
            return (sq_tmp if c % 4 >= 2 else act_tmp)[:, c % 2, :]

        @block.sync
        def _(sp):
            def load(n, src, cols=SLAB):
                r = R_OF[n]
                if r >= 2:
                    sp.wait_ge(lo_done, N_OF[r - 2] + 1)
                sp.dma_start(raw[r % 2][:, 0:cols], src).then_inc(raw_s[r % 2], 16)

            def load_ada(a):
                sp.wait_ge(ada_step, 4 * a)
                sp.dma_start(ada_raw[:, :, :].rearrange("p k n -> p (k n)"), ada_in[a, :, :]).then_inc(ada_s, 16)

            def up_loads(j, i, ada):
                for s in range(2):
                    sp.wait_ge(lo_done, N_UP[j] + 2 * i + s + 1)
                    sp.dma_start(raw[s][:, :], up_in[KF * j + 2 * i + 2 + s, :, :]).then_inc(raw_s[s], 16)
                    if ada:
                        load_ada(2 * (Q_FFN[j] + i) + s)

            def ffn_loads(j):
                nb = Q_BODIES[j]
                with sp.Fori(0, min(nb, 10)) if nb else ExitStack() as i:
                    if nb:
                        up_loads(j, i, True)
                if nb < 10:
                    with sp.Fori(nb, 10) as i:
                        up_loads(j, i, False)
                for s in range(2):
                    load(N_DOWN[j] + s, down_in[2 * KD * j + s, :, :], DOWN)
                    if nb == 11:
                        load_ada(2 * (Q_FFN[j] + 10) + s)
                with sp.Fori(1, KD) as i:
                    for s in range(2):
                        sp.wait_ge(lo_done, N_DOWN[j] + 2 * i - 1 + s)
                        sp.dma_start(raw[s][:, 0:DOWN], down_in[2 * KD * j + 2 * i + s, :, :]).then_inc(raw_s[s], 16)

            sp.dma_start(vec[:, :], vec_in).then_inc(vec_s, 16)
            sp.dma_start(ident[:, :], con_in[:, 0, :]).then_inc(vec_s, 16)
            for a in range(12):
                if a >= 6:
                    sp.wait_ge(ada_step, 4 * (a - 5))
                sp.dma_start(stage[a % 6][:, :, :].rearrange("p k n -> p (k n)"), ada_in[a, :, :]) \
                    .then_inc(stage_s[a % 6], 16)
                if a == 5:
                    for i in range(2):
                        sp.dma_start(x[:, 4 * i:4 * i + 4, :], x_in[:, 4 * i:4 * i + 4, :]).then_inc(x_in_s[i], 16)
            for s in range(2):
                load(N_UP[0] + s, up_in[s, :, :])
            ffn_loads(0)
            for c in range(KD):
                load(CIN[c], mix_in[c, :, :])
                if c == 1:
                    sp.wait_ge(x_done, KD)
                    sp.dma_start(dw[:, :, :], dw_in).then_inc(dw_s, 16)
            for i in range(2):
                load(N_OUT + i, mix_in[8 + i, :, :])
            for i in range(4):
                load_ada(2 * Q_OUT + i)
                if i < 2:
                    load(N_OUT + 2 + i, mix_in[10 + i, :, :])
                else:
                    load(N_UP[1] + i - 2, up_in[KF + i - 2, :, :])
            for i in range(4, 6):
                load_ada(2 * Q_OUT + i)
            ffn_loads(1)
            for s in range(2):
                load(N_UP[2] + s, up_in[2 * KF + s, :, :])
            ffn_loads(2)
            for s in range(12):
                load(N_QKV + s, mix_in[12 + s, :, :])
                if s == 1:
                    sp.wait_ge(x_done, 4 * KD)
                    sp.dma_start(con_f[:, :, :], con_in).then_inc(con_s, 16)
                    sp.dma_start(ind[:, :, :], ind_in).then_inc(con_s, 16)
                    sp.dma_start(sel_f[:, :, :], sel_in).then_inc(con_s, 16)
            load(N_WO, mix_in[24, :, :])
            sp.wait_ge(av_done, HEADS)
            for i in range(1, 4):
                load(N_WO + i, mix_in[24 + i, :, :])
            for s in range(2):
                load(N_UP[3] + s, up_in[3 * KF + s, :, :])
            ffn_loads(3)
            for d in range(KD):
                sp.wait_ge(x_done, 5 * KD + d + 1)
                sp.dma_start(out[:, d, :], x[:, d, :]).then_inc(out_s, 16)
            sp.wait_ge(out_s, 16 * KD)

        @block.gpsimd
        def _(pool):
            pool.memset(ones[:, :], 1.0).then_inc(ones_done, 1)

            def squares(m, c):
                if c == 0:
                    return
                pool.wait_ge(sq_done, KD * m + c + 1)
                if c > 1:
                    pool.wait_ge(ss_step, 7 * m + c - 1)
                a = sq_tmp[:, 0, :] if c == 1 else ss[:, :]
                pool.tensor_tensor(ss[:, :], a, sq_tmp[:, c % 2, :], ALU.add).then_inc(ss_step, 1)

            for c in range(KD):
                squares(0, c)
            for c in range(KD):
                squares(1, c)

            pool.wait_ge(dw_s, 16)
            for c in range(KD):
                if c >= 1:
                    pool.wait_ge(lo_done, CTAP[c - 1] + 1)
                pool.tensor_tensor(
                    diag[:, :].rearrange("p (t m) -> p t m", t=TP),
                    ident[:, :].rearrange("p (t m) -> p t m", t=1).broadcast_to((P, TP, P)),
                    dw[:, c, TV:W].rearrange("p (t m) -> p t m", m=1).broadcast_to((P, TP, P)),
                    ALU.mult).then_inc(diag_done, 1)
                if c >= 2:
                    pool.wait_ge(v_done, c)
                    if c > 2:
                        pool.wait_ge(vsum_step, c - 2)
                    a = v[:, 0, :] if c == 2 else v_sum[:, :]
                    pool.tensor_tensor(v_sum[:, :], a, v[:, c - 1, :], ALU.add).then_inc(vsum_step, 1)
            pool.wait_ge(v_done, KD)
            pool.wait_ge(vsum_step, KD - 2)
            pool.tensor_tensor(v_sum[:, :], v_sum[:, :], v[:, KD - 1, :], ALU.add).then_inc(vsum_step, 1)
            for m in range(2, 6):
                for c in range(KD):
                    squares(m, c)

            def sp_low(t):
                pool.wait_ge(sphi_done, t + 1)
                if t >= 1:
                    pool.wait_ge(cum_done, t)
                pool.tensor_tensor(sp_lo[:, :], sp_abs[:, t % 2, :], f32(sp_hi[:, :]), ALU.subtract) \
                    .then_inc(splo_done, 1)

            def a_low(t):
                pool.wait_ge(ahi_done, t + 1)
                if t >= 1:
                    pool.wait_ge(av_done, t)
                pool.tensor_tensor(a_lo[:, :], a_f[:, :], f32(a_hi[:, :]), ALU.subtract).then_inc(alo_done, 1)

            for t in range(HEADS):
                sp_low(t)
                if t >= 1:
                    a_low(t - 1)
            a_low(HEADS - 1)
            for c in range(KD):
                squares(6, c)

        @block.scalar
        def _(act):
            def hi(n, cols=SLAB):
                if n in CTAP:
                    act.wait_ge(diag_done, CTAP.index(n) + 1)
                    src = diag[:, 0:cols]
                else:
                    r = R_OF[n]
                    act.wait_ge(raw_s[r % 2], 16 * (r // 2 + 1))
                    src = raw[r % 2][:, 0:cols]
                if n >= 2:
                    act.wait_ge(slab_done, n - 1)
                act.activation(wsp[n % 2][:, 0, 0:cols], src, ACT.Copy).then_inc(hi_done, 1)

            def square(m, c, src, ready, value):
                act.wait_ge(ready, value)
                if c >= 2:
                    act.wait_ge(ss_step, 7 * m + max(1, c - 2))
                act.activation(sq_tmp[:, c % 2, :], src, ACT.Square).then_inc(sq_done, 1)

            def table():
                act.wait_ge(ones_done, 1)
                act.activation(st[:, 20:21], ones[:, 0:1], ACT.Sqrt)

            def root(m):
                act.wait_ge(vec_step, 4 * m + 1)
                act.activation(st[:, 4:8], st[:, 0:4], ACT.Sqrt).then_inc(sqrt_done, 1)

            def h_his(m, layer, sub):
                for c in range(KD):
                    act.wait_ge(t_done, KD * m + c + 1)
                    act.activation(h_hi[:, c, :], t_buf(c), ACT.Identity,
                                   bias=mod(layer, sub, 0, c, 1)).then_inc(hhi_done, 1)

            def up_step(j, i, s, split=True):
                n = N_UP[j] + 2 * i + s
                act.wait_ge(slab_done, n + 1)
                act.activation(act_tmp[:, s, :], pair[s][0], ACT.Silu).then_inc(silu_done, 1)
                act.wait_ge(g_full, KF * j + 2 * i + s + 1)
                act.activation(g_hi[:, 2 * i + s, :], act_tmp[:, s, :], ACT.Copy).then_inc(ghi_done, 1)
                if split:
                    act.wait_ge(raw_s[s], 16 * (R_OF[N_UP[j]] // 2 + 2) + 16 * i)
                    act.activation(wsp[s][:, 0, :], raw[s][:, :], ACT.Copy).then_inc(hi_done, 1)

            def ffn(j, m, nxt, last=False):
                with act.Fori(0, 10) as i:
                    for s in range(2):
                        up_step(j, i, s)
                for s in range(2):
                    up_step(j, 10, s, split=False)
                    hi(N_DOWN[j] + s, DOWN)
                if not last:
                    table()
                for d in range(KD):
                    if d < KD - 1:
                        hi(N_DOWN[j] + 2 * d + 2, DOWN)
                        hi(N_DOWN[j] + 2 * d + 3, DOWN)
                    elif not last:
                        hi(nxt)
                    if not last:
                        square(m, d, x[:, d, :], x_done, KD * max(0, m - 2) + d + 1)
                if not last:
                    hi(nxt + 1)

            act.wait_ge(mod_done, 2)
            act.activation(e_col[:, :], e_pre[:, :], ACT.Silu).then_inc(e_done, 1)
            for c in range(KD):
                square(0, c, x[:, c, :], x_in_s[c // 4], 16)
            table()
            root(0)
            hi(N_UP[0])
            hi(N_UP[0] + 1)
            h_his(0, 0, 0)
            ffn(0, 1, N_CONV)
            root(1)
            h_his(1, 0, 1)

            for c in range(KD):
                act.wait_ge(slab_done, CIN[c] + 1)
                act.activation(act_tmp[:, 0, :], pair[0][1], ACT.Sigmoid, bias=vcol("b_in", KD + c)) \
                    .then_inc(sig_done, 1)
                act.wait_ge(u_done, c + 1)
                if c == 0:
                    act.wait_ge(pad_done, 3)
                act.activation(u_hi[:, c % 2, W - 1:], u[:, c % 2, W - 1:], ACT.Copy).then_inc(uhi_done, 1)
                if c == 0:
                    hi(CTAP[0], DIAG)
                    hi(CIN[2])
                elif c < KD - 2:
                    hi(CTAP[c], DIAG)
                    hi(CIN[c + 2])
                elif c == KD - 2:
                    hi(CTAP[c], DIAG)
                else:
                    hi(CTAP[c], DIAG)
                    hi(N_OUT)
                    hi(N_OUT + 1)
            for c in range(KD):
                square(2, c, v[:, c, :], vc_done, c + 1)
            table()
            root(2)
            for c in range(KD):
                act.wait_ge(t_done, KD * 2 + c + 1)
                act.activation(t_buf(c), t_buf(c), ACT.Silu, scale=vcol("ln_g", c),
                               bias=vcol("ln_b", c)).then_inc(yact_done, 1)
                act.wait_ge(yact_done, c + 1)
                act.activation(h_hi[:, c, :], t_buf(c), ACT.Copy).then_inc(hhi_done, 1)

            def out_steps(n0, m, nxt):
                for i in range(4):
                    if i < 2:
                        hi(n0 + i + 2)
                    elif i == 2:
                        hi(nxt)
                    for d in (2 * i, 2 * i + 1):
                        square(m, d, x[:, d, :], x_done, KD * (m - 2) + d + 1)
                hi(nxt + 1)

            table()
            out_steps(N_OUT, 3, N_UP[1])
            root(3)
            h_his(3, 0, 2)
            ffn(1, 4, N_UP[2])
            root(4)
            h_his(4, 1, 0)
            ffn(2, 5, N_QKV)
            root(5)
            h_his(5, 1, 1)

            def y_root(g):
                act.wait_ge(yv_done, g + 1)
                act.activation(y[:, 1, :], y[:, 0, :], ACT.Sqrt).then_inc(ysq_done, 1)

            for s in range(12):
                if s < 11:
                    hi(N_QKV + s + 2)
                if s < 8:
                    for c in (2 * s, 2 * s + 1):
                        act.wait_ge(qk_done, c + 1)
                        if c >= 2:
                            act.wait_ge(ind_done, c - 1)
                        act.activation(sq_tmp[:, c % 2, :], qk[:, c, :], ACT.Square).then_inc(qksq_done, 1)
                else:
                    act.wait_ge(slab_done, N_QKV + s + 1)
                    for b in range(2):
                        act.activation(v_hi[:, 2 * b:2 * b + 2, 256 * (s - 8):256 * (s - 7)],
                                       pair[s % 2][b].rearrange("p (c n) -> p c n", c=2), ACT.Copy) \
                            .then_inc(vhi_done, 1)
                if s == 4:
                    y_root(0)
                if s == 8:
                    y_root(1)

            def o_high(t):
                act.wait_ge(av_done, t + 1)
                q = slice(HD * (t % 2), HD * (t % 2) + HD)
                act.activation(h_hi[q, t // 2, :], ps[q, 6 + t % 2, :], ACT.Copy).then_inc(ohi_done, 1)

            def weights(t):
                act.wait_ge(cum_done, t + 1)
                if t >= 1:
                    act.wait_ge(ahi_done, t)
                    act.wait_ge(alo_done, t)
                act.activation(a_f[:, :], zps[:, 3 * S * (t % 2):3 * S * (t % 2) + QL], ACT.Exp) \
                    .then_inc(a_done, 1)

            act.add_instruction(mybir.InstLoadActFuncSet(
                name=nc.get_next_instruction_name(), engine=mybir.EngineType.Activation, act_func_set_id=EXP_LN_SET))
            for t in range(HEADS):
                z = zps[:, 3 * S * (t % 2):3 * S * (t % 2) + QL]
                w = sp_abs[:, t % 2, :]
                act.wait_ge(z_done, t + 1)
                if t == 0:
                    act.wait_ge(slab_done, N_QKV + 12)
                if t >= 2:
                    act.wait_ge(splo_done, t - 1)
                act.activation(w, z, ACT.Abs).then_inc(ln_step, 1)
                act.wait_ge(ln_step, 3 * t + 1)
                act.activation(w, w, ACT.Exp, scale=-1.0).then_inc(ln_step, 1)
                act.wait_ge(ln_step, 3 * t + 2)
                act.activation(w, w, ACT.Ln, bias=ones[:, 0:1]).then_inc(ln_step, 1)
                if t >= 1:
                    weights(t - 1)
                if t >= 2:
                    o_high(t - 2)
            weights(HEADS - 1)
            o_high(HEADS - 2)
            o_high(HEADS - 1)
            hi(N_WO + 1)
            table()
            out_steps(N_WO, 6, N_UP[3])
            root(6)
            h_his(6, 1, 2)
            ffn(3, None, None, last=True)

        @block.vector
        def _(dve):
            def lo(n, cols=SLAB):
                dve.wait_ge(hi_done, n + 1)
                src = diag[:, 0:cols] if n in CTAP else raw[R_OF[n] % 2][:, 0:cols]
                dve.tensor_tensor(wsp[n % 2][:, 1, 0:cols], src, f32(wsp[n % 2][:, 0, 0:cols]), ALU.subtract) \
                    .then_inc(lo_done, 1)

            def ada_half(q, s, buf, acc):
                for k in range(4):
                    a = 8 * q + 4 * s + k
                    col = 4 * s + k
                    w = e_col[:, col:col + 1] if not isinstance(q, int) or q >= 2 else vcol("c", col)
                    if s == 0 and k == 0:
                        dve.tensor_scalar(acc, buf[:, k, :], w, None, ALU.mult).then_inc(ada_step, 1)
                    else:
                        dve.wait_ge(ada_step, a)
                        dve.scalar_tensor_tensor(out=acc, in0=buf[:, k, :], scalar=w, in1=acc, op0=ALU.mult,
                                                 op1=ALU.add).then_inc(ada_step, 1)

            def ada_take(q):
                dve.wait_ge(ada_sum, q + 1)
                if isinstance(q, int) and q < 2:
                    dst, b = e_pre[:, 4 * q:4 * q + 4], vcol("cond_b", 4 * q, 4)
                else:
                    dst = mods[:, :].rearrange("p (g n) -> p g n", n=4)[:, q - 2, :]
                    b = vcol("ada_b", 0, 144).rearrange("p (g n) -> p g n", n=4)[:, q - 2, :]
                dve.tensor_tensor(dst, ada_ps, b, ALU.add).then_inc(mod_done, 1)

            def factor(m):
                vv, sd, y0, y1 = st[:, 0:4], st[:, 4:8], st[:, 8:12], st[:, 16:20]
                dve.wait_ge(stat_done, m + 1)
                dve.tensor_scalar(vv, row[:, 0:4], 1.0 / D, EPS, ALU.mult, ALU.add).then_inc(vec_step, 1)
                dve.wait_ge(sqrt_done, m + 1)
                dve.reciprocal(y0, sd).then_inc(vec_step, 1)
                dve.wait_ge(vec_step, 4 * m + 2)
                dve.tensor_tensor(y1, y0, y0, ALU.mult).then_inc(vec_step, 1)
                dve.wait_ge(vec_step, 4 * m + 3)
                dve.scalar_tensor_tensor(out=y1, in0=y1, scalar=-0.5, in1=vv, op0=ALU.mult, op1=ALU.mult) \
                    .then_inc(vec_step, 1)
                dve.wait_ge(vec_step, 4 * m + 4)
                dve.scalar_tensor_tensor(out=sd, in0=y1, scalar=1.5, in1=y0, op0=ALU.add, op1=ALU.mult) \
                    .then_inc(fac_step, 1)
                dve.wait_ge(fac_step, m + 1)
                dve.tensor_tensor(
                    sq_tmp[:, 0, :].rearrange("p (c m) -> p c m", c=4),
                    ident[:, :].rearrange("p (c m) -> p c m", c=1).broadcast_to((P, 4, P)),
                    sd.rearrange("p (c m) -> p c m", m=1).broadcast_to((P, 4, P)),
                    ALU.mult).then_inc(rdiag_done, 1)

            def h_lows(m, layer, sub):
                dve.wait_ge(mod_done, 2 + 18 * layer + 6 * sub + 4)
                dve.scalar_tensor_tensor(out=gs[:, :], in0=mod(layer, sub, 1), scalar=1.0,
                                         in1=vcol("norm_g", (3 * layer + sub) * KD, KD), op0=ALU.add,
                                         op1=ALU.mult).then_inc(gs_done, 1)
                factor(m)
                dve.wait_ge(gs_done, (m if m < 2 else m - 1) + 1)
                dve.wait_ge(row_done, m + 1)
                for c in range(KD + 1):
                    if c < KD:
                        if c >= 4:
                            dve.wait_ge(h_done, KD * m + c - 3)
                        dve.scalar_tensor_tensor(out=t_buf(c), in0=x[:, c, :], scalar=gs[:, c:c + 1],
                                                 in1=row, op0=ALU.mult, op1=ALU.mult).then_inc(t_done, 1)
                    if c >= 1:
                        b = c - 1
                        dve.wait_ge(hhi_done, KD * m + b + 1)
                        dve.scalar_tensor_tensor(out=h_lo[:, b, :], in0=t_buf(b),
                                                 scalar=mod(layer, sub, 0, b, 1), in1=f32(h_hi[:, b, :]),
                                                 op0=ALU.add, op1=ALU.subtract).then_inc(h_done, 1)

            def gate(layer, sub, k, factor_):
                dve.wait_ge(mod_done, 2 + 18 * layer + 6 * sub + 6)
                dve.tensor_scalar(gt[:, :], mod(layer, sub, 2), 1.0, factor_, ALU.add, ALU.mult).then_inc(gate_done, 1)
                dve.wait_ge(gate_done, k)

            def x_add(d, src):
                dve.scalar_tensor_tensor(out=x[:, d, :], in0=src, scalar=gt[:, d:d + 1], in1=x[:, d, :],
                                         op0=ALU.mult, op1=ALU.add).then_inc(x_done, 1)

            def up_step(j, i, s, ada, split=True, take=True):
                n = N_UP[j] + 2 * i + s
                f = KF * j + 2 * i + s
                dve.wait_ge(silu_done, f + 1)
                dve.tensor_tensor(act_tmp[:, s, :], act_tmp[:, s, :], pair[s][1], ALU.mult).then_inc(g_full, 1)
                dve.wait_ge(ghi_done, f + 1)
                dve.tensor_tensor(g_lo[:, 2 * i + s, :], act_tmp[:, s, :], f32(g_hi[:, 2 * i + s, :]),
                                  ALU.subtract).then_inc(g_done, 1)
                if split:
                    dve.wait_ge(hi_done, n + 3)
                    dve.tensor_tensor(wsp[s][:, 1, :], raw[s][:, :], f32(wsp[s][:, 0, :]), ALU.subtract) \
                        .then_inc(lo_done, 1)
                else:
                    lo(N_DOWN[j] + s, DOWN)
                if ada:
                    q = Q_FFN[j] + i
                    if s == 0 and take:
                        ada_take(q - 1)
                    dve.wait_ge(ada_s, 16 * (2 * q - 11 + s))
                    ada_half(q, s, ada_raw, ada_acc[:, :])

            def ffn(j, k, layer, sub, nxt, last=False):
                nb = Q_BODIES[j]
                if nb:
                    for s in range(2):
                        up_step(j, 0, s, True, take=False)
                    with dve.Fori(1, min(nb, 10)) as i:
                        for s in range(2):
                            up_step(j, i, s, True)
                if nb < 10:
                    with dve.Fori(nb, 10) as i:
                        for s in range(2):
                            up_step(j, i, s, False)
                    if nb:
                        ada_take(Q_FFN[j] + nb - 1)
                for s in range(2):
                    up_step(j, 10, s, nb == 11, split=False)
                gate(layer, sub, k, 0.5)
                for d in range(KD):
                    if d < KD - 1:
                        lo(N_DOWN[j] + 2 * d + 2, DOWN)
                    elif not last:
                        lo(nxt)
                    dve.wait_ge(slab_done, N_DOWN[j] + 2 * d + 2)
                    x_add(d, down_ps[d % 2])
                    if d < KD - 1:
                        lo(N_DOWN[j] + 2 * d + 3, DOWN)
                if nb == 11:
                    ada_take(Q_FFN[j] + 10)

            dve.wait_ge(vec_s, 32)
            for q in range(6):
                for s in range(2):
                    a = 2 * q + s
                    dve.wait_ge(stage_s[a % 6], 16 * (a // 6 + 1))
                    if q == 2 and s == 0:
                        ada_take(1)
                        dve.wait_ge(e_done, 1)
                    ada_half(q, s, stage[a % 6], act_tmp[:, q % 2, :])
                    if s == 0 and q >= 1 and q != 2:
                        ada_take(q - 1)
            ada_take(5)
            h_lows(0, 0, 0)
            lo(N_UP[0])
            lo(N_UP[0] + 1)
            ffn(0, 1, 0, 0, N_CONV)
            h_lows(1, 0, 1)
            lo(N_CONV + 1)

            for b in range(2):
                dve.memset(u[:, b, 0:W - 1], 0.0)
                dve.memset(f32(u_hi[:, b, 0:W - 1]), 0.0)
                last = dve.memset(f32(u_lo[:, b, 0:W - 1]), 0.0)
                last.then_inc(pad_done, 1)
            dve.drain().then_inc(pad_done, 1)
            dve.wait_ge(pad_done, 3)

            def taps(c, lo_t, hi_t):
                for t in range(lo_t, hi_t):
                    src = u[:, c % 2, t:t + S]
                    w = dw[:, c, t:t + 1]
                    dst = v[:, c, :] if t % 2 == 0 else v_odd[:, :]
                    if t == 0:
                        ins = dve.tensor_scalar(dst, src, w, vcol("dw_b", c), ALU.mult, ALU.add)
                    elif t == 1:
                        if c >= 1:
                            dve.wait_ge(vodd_done, c)
                        ins = dve.tensor_scalar(dst, src, w, None, ALU.mult)
                    else:
                        dve.wait_ge(tap_step, TV * c + t - 1)
                        ins = dve.scalar_tensor_tensor(out=dst, in0=src, scalar=w, in1=dst, op0=ALU.mult, op1=ALU.add)
                    ins.then_inc(tap_step, 1)

            def combine(c):
                dve.wait_ge(slab_done, CTAP[c] + 1)
                dve.wait_ge(vodd_done, c + 1)
                dve.tensor_tensor(v[:, c, :], v[:, c, :], pair[1][0], ALU.add).then_inc(v_done, 1)

            dve.wait_ge(dw_s, 16)
            for c in range(KD):
                dve.wait_ge(sig_done, c + 1)
                dve.scalar_tensor_tensor(out=u[:, c % 2, W - 1:], in0=pair[0][0], scalar=vcol("b_in", c),
                                         in1=act_tmp[:, 0, :], op0=ALU.add, op1=ALU.mult).then_inc(u_done, 1)
                dve.wait_ge(uhi_done, c + 1)
                dve.tensor_tensor(u_lo[:, c % 2, W - 1:], u[:, c % 2, W - 1:], f32(u_hi[:, c % 2, W - 1:]),
                                  ALU.subtract).then_inc(ulo_done, 1)
                if c >= 1:
                    taps(c, 0, TV // 2)
                    combine(c - 1)
                    lo(CTAP[c], DIAG)
                    if c < KD - 2:
                        lo(CIN[c + 2])
                    taps(c, TV // 2, TV)
                else:
                    lo(CTAP[0], DIAG)
                    lo(CIN[2])
                    taps(c, 0, TV)
                dve.wait_ge(tap_step, TV * (c + 1))
                dve.tensor_tensor(v[:, c, :], v[:, c, :], v_odd[:, :], ALU.add).then_inc(vodd_done, 1)
            combine(KD - 1)
            lo(N_OUT)
            dve.wait_ge(mean_done, 1)
            for c in range(KD):
                dve.scalar_tensor_tensor(out=v[:, c, :], in0=row, scalar=-1.0 / D, in1=v[:, c, :], op0=ALU.mult,
                                         op1=ALU.add).then_inc(vc_done, 1)
            lo(N_OUT + 1)
            factor(2)
            dve.wait_ge(row_done, 3)
            for c in range(KD + 1):
                if c < KD:
                    if c >= 4:
                        dve.wait_ge(h_done, KD * 2 + c - 3)
                    dve.tensor_tensor(t_buf(c), v[:, c, :], row, ALU.mult).then_inc(t_done, 1)
                if c >= 1:
                    b = c - 1
                    dve.wait_ge(hhi_done, KD * 2 + b + 1)
                    dve.tensor_tensor(h_lo[:, b, :], t_buf(b), f32(h_hi[:, b, :]), ALU.subtract) \
                        .then_inc(h_done, 1)
            gate(0, 1, 2, 1.0)
            for i in range(4):
                if i < 2:
                    lo(N_OUT + i + 2)
                elif i == 2:
                    lo(N_UP[1])
                dve.wait_ge(slab_done, N_OUT + i + 1)
                if i >= 1:
                    dve.wait_ge(x_done, KD + 2 * i)
                for b in range(2):
                    d = 2 * i + b
                    dve.tensor_scalar(act_tmp[:, b, :], pair[i % 2][b], vcol("b_out", d), gt[:, d:d + 1], ALU.add,
                                      ALU.mult).then_inc(bo_step, 1)
                for b in range(2):
                    d = 2 * i + b
                    dve.wait_ge(bo_step, d + 1)
                    dve.tensor_tensor(x[:, d, :], x[:, d, :], act_tmp[:, b, :], ALU.add).then_inc(x_done, 1)
                if i < 3:
                    q = Q_OUT + i
                    for s in range(2):
                        dve.wait_ge(ada_s, 16 * (2 * q - 11 + s))
                        ada_half(q, s, ada_raw, ada_acc[:, :])
                    ada_take(q)
            h_lows(3, 0, 2)
            lo(N_UP[1] + 1)
            ffn(1, 3, 0, 2, N_UP[2])
            h_lows(4, 1, 0)
            lo(N_UP[2] + 1)
            ffn(2, 4, 1, 0, N_QKV)
            h_lows(5, 1, 1)
            lo(N_QKV + 1)

            dve.wait_ge(con_s, 48)
            dve.tensor_copy(con[:, :, :], con_f[:, :, :]).then_inc(conr_done, 1)
            dve.tensor_copy(sel[:, :, :], sel_f[:, :, :]).then_inc(conr_done, 1)

            def head_factors(g):
                dve.wait_ge(ind_done, KD * (g + 1))
                dve.tensor_scalar(y[:, 0, :], ps[0:32, 6 + g, :], 1.0 / HD, EPS, ALU.mult, ALU.add).then_inc(yv_done, 1)
                dve.wait_ge(ysq_done, g + 1)
                dve.reciprocal(y[:, 2, :], y[:, 1, :]).then_inc(yn_step, 1)
                dve.wait_ge(yn_step, 4 * g + 1)
                dve.tensor_tensor(y[:, 3, :], y[:, 2, :], y[:, 2, :], ALU.mult).then_inc(yn_step, 1)
                dve.wait_ge(yn_step, 4 * g + 2)
                dve.scalar_tensor_tensor(out=y[:, 3, :], in0=y[:, 3, :], scalar=-0.5, in1=y[:, 0, :], op0=ALU.mult,
                                         op1=ALU.mult).then_inc(yn_step, 1)
                dve.wait_ge(yn_step, 4 * g + 3)
                dve.scalar_tensor_tensor(out=y[:, 3, :], in0=y[:, 3, :], scalar=1.5, in1=y[:, 2, :], op0=ALU.add,
                                         op1=ALU.mult).then_inc(yn_step, 1)
                dve.wait_ge(yn_step, 4 * g + 4)
                if g == 1:
                    dve.wait_ge(bc_done, KD)
                dve.tensor_copy(y_hi[:, :], y[:, 3, :]).then_inc(y_done, 1)
                dve.wait_ge(y_done, 2 * g + 1)
                dve.tensor_tensor(y_lo[:, :], y[:, 3, :], f32(y_hi[:, :]), ALU.subtract).then_inc(y_done, 1)

            def normalise(b):
                dve.wait_ge(bc_done, b + 1)
                dve.scalar_tensor_tensor(out=qk[:, b, :], in0=qk[:, b, :], scalar=vcol("qk_g", b // KD),
                                         in1=down_ps[b % 2], op0=ALU.mult, op1=ALU.mult).then_inc(qkn_done, 1)

            for s in range(12):
                n = N_QKV + s
                dve.wait_ge(slab_done, n + 1)
                if s < 8:
                    for b in range(2):
                        dve.tensor_copy(qk[:, 2 * s + b, :], pair[s % 2][b]).then_inc(qk_done, 1)
                else:
                    for b in range(2):
                        dve.wait_ge(vhi_done, 2 * (s - 8) + b + 1)
                        at = (slice(None), slice(2 * b, 2 * b + 2), slice(256 * (s - 8), 256 * (s - 7)))
                        dve.tensor_tensor(v_lo[at], pair[s % 2][b].rearrange("p (c n) -> p c n", c=2),
                                          f32(v_hi[at]), ALU.subtract).then_inc(vlo_done, 1)
                if s < 11:
                    lo(n + 2)
                if s == 4:
                    head_factors(0)
                if s == 8:
                    normalise(6)
                    normalise(7)
                    head_factors(1)
                elif s >= 5:
                    for b in range(2 * (s - 5), 2 * (s - 5) + 2 if s < 11 else 16):
                        normalise(b)

            def split_qk(c):
                b = c % 2
                if c >= 2:
                    dve.wait_ge(z_done, 2 * c - 2)
                if c == 0:
                    dve.wait_ge(qkn_done, 16)
                dve.tensor_scalar(qk_s[:, b, 0, :], qk[:, c, :], HD ** -0.5, None, ALU.mult).then_inc(qks_step, 1)
                dve.tensor_copy(qk_s[:, b, 2, :], qk[:, KD + c, :]).then_inc(qks_step, 1)
                dve.wait_ge(qks_step, 4 * c + 1)
                dve.scalar_tensor_tensor(out=qk_s[:, b, 1, :], in0=qk[:, c, :], scalar=HD ** -0.5,
                                         in1=f32(qk_s[:, b, 0, :]), op0=ALU.mult, op1=ALU.subtract) \
                    .then_inc(qks_step, 1)
                dve.wait_ge(qks_step, 4 * c + 2)
                dve.tensor_tensor(qk_s[:, b, 3, :], qk[:, KD + c, :], f32(qk_s[:, b, 2, :]), ALU.subtract) \
                    .then_inc(qks_step, 1)

            def softplus(t):
                w = sp_abs[:, t % 2, :]
                dve.wait_ge(ln_step, 3 * t + 3)
                dve.scalar_tensor_tensor(out=w, in0=zps[:, 3 * S * (t % 2):3 * S * (t % 2) + QL], scalar=0.0, in1=w,
                                         op0=ALU.max, op1=ALU.add).then_inc(sp_done, 1)
                dve.wait_ge(sp_done, t + 1)
                if t >= 1:
                    dve.wait_ge(cum_done, t)
                dve.tensor_copy(sp_hi[:, :], w).then_inc(sphi_done, 1)

            def a_high(t):
                dve.wait_ge(a_done, t + 1)
                if t >= 1:
                    dve.wait_ge(av_done, t)
                dve.tensor_copy(a_hi[:, :], a_f[:, :]).then_inc(ahi_done, 1)

            def o_low(t):
                q = slice(HD * (t % 2), HD * (t % 2) + HD)
                dve.wait_ge(ohi_done, t + 1)
                dve.tensor_tensor(h_lo[q, t // 2, :], ps[q, 6 + t % 2, :], f32(h_hi[q, t // 2, :]), ALU.subtract) \
                    .then_inc(o_done, 1)

            split_qk(0)
            for t in range(HEADS):
                softplus(t)
                if t >= 1:
                    a_high(t - 1)
                if t >= 2:
                    o_low(t - 2)
                if t % 2 == 0 and t // 2 + 1 < KD:
                    split_qk(t // 2 + 1)
            a_high(HEADS - 1)
            o_low(HEADS - 2)
            o_low(HEADS - 1)
            gate(1, 1, 5, 1.0)
            lo(N_WO + 1)
            for i in range(4):
                if i < 2:
                    lo(N_WO + i + 2)
                elif i == 2:
                    lo(N_UP[3])
                dve.wait_ge(slab_done, N_WO + i + 1)
                for b in range(2):
                    x_add(2 * i + b, pair[i % 2][b])
            h_lows(6, 1, 2)
            lo(N_UP[3] + 1)
            ffn(3, 6, 1, 2, None, last=True)

        @block.tensor
        def _(pe):
            def triple(dst, a_hi_, a_lo_, b_hi_, b_lo_, start, stop):
                pe.matmul(dst, a_hi_, b_hi_, start=start, stop=False, skip_group_check=True)
                pe.matmul(dst, a_hi_, b_lo_, start=False, stop=False, skip_group_check=True)
                return pe.matmul(dst, a_lo_, b_hi_, start=False, stop=stop, skip_group_check=True)

            def two_chunks(slot, banks, k0=None):
                w = wsp[slot]
                for k in range(KD):
                    if k0 is not None:
                        pe.wait_ge(h_done, k0 + k + 1)
                    for b in range(2):
                        at = slice((2 * k + b) * P, (2 * k + b + 1) * P)
                        last = triple(banks[b], w[:, 0, at], w[:, 1, at], h_hi[:, k, :], h_lo[:, k, :],
                                      k == 0, k == KD - 1)
                return last

            def stats(m):
                pe.wait_ge(ss_step, 7 * (m + 1))
                for c in range(4):
                    last = pe.matmul(row[:, c:c + 1], ss[:, c * P:(c + 1) * P], ones[:, 0:1], start=True, stop=True)
                last.then_inc(stat_done, 1)
                pe.wait_ge(rdiag_done, m + 1)
                pe.matmul(row, ones[:, :], sq_tmp[:, 0, :], start=True, stop=True).then_inc(row_done, 1)

            def ada_reduce(q, acc):
                pe.wait_ge(ada_step, 8 * q + 8)
                for c in range(4):
                    last = pe.matmul(ada_ps[:, c:c + 1], acc[:, c * P:(c + 1) * P], ones[:, 0:1], start=True, stop=True)
                last.then_inc(ada_sum, 1)

            def up_step(j, i, s, m, ada):
                pe.wait_ge(lo_done, N_UP[j] + 2 * i + s + 1)
                two_chunks(s, pair[s], m if m is None else KD * m).then_inc(slab_done, 1)
                if ada and s == 0:
                    ada_reduce(Q_FFN[j] + i - 1, ada_acc)

            def ffn(j, m):
                nb = Q_BODIES[j]
                up_step(j, 0, 0, m, False)
                up_step(j, 0, 1, None, False)
                if nb:
                    with pe.Fori(1, min(nb + 1, 11)) as i:
                        for s in range(2):
                            up_step(j, i, s, None, True)
                if nb < 11:
                    with pe.Fori(nb + 1, 11) as i:
                        for s in range(2):
                            up_step(j, i, s, None, False)
                with pe.Fori(0, KD // 2) as i:
                    for s in range(2):
                        for half in range(2):
                            pe.wait_ge(lo_done, N_DOWN[j] + 4 * i + 2 * s + half + 1)
                            pe.wait_ge(g_done, KF * j + HF * (half + 1))
                            w = wsp[half]
                            for k in range(HF):
                                at = slice(k * P, (k + 1) * P)
                                f = HF * half + k
                                last = triple(down_ps[s], w[:, 0, at], w[:, 1, at], g_hi[:, f, :], g_lo[:, f, :],
                                              f == 0, f == KF - 1)
                            last.then_inc(slab_done, 1)
                if nb == 11:
                    ada_reduce(Q_FFN[j] + 10, ada_acc)

            pe.wait_ge(ones_done, 1)
            for q in range(6):
                if q >= 1:
                    pe.wait_ge(mod_done, q)
                ada_reduce(q, act_tmp[:, q % 2, :])
            stats(0)
            ffn(0, 0)
            stats(1)

            def conv_in(c):
                pe.wait_ge(lo_done, CIN[c] + 1)
                if c >= 1:
                    pe.wait_ge(u_done, c)
                two_chunks(CIN[c] % 2, pair[0], KD if c == 0 else None).then_inc(slab_done, 1)

            def conv_taps(c):
                n = CTAP[c]
                pe.wait_ge(lo_done, n + 1)
                pe.wait_ge(ulo_done, c + 1)
                if c >= 1:
                    pe.wait_ge(v_done, c)
                w = wsp[n % 2]
                for t in range(TP):
                    at = slice(t * P, (t + 1) * P)
                    last = triple(pair[1][0], w[:, 0, at], w[:, 1, at], u_hi[:, c % 2, TV + t:TV + t + S],
                                  u_lo[:, c % 2, TV + t:TV + t + S], t == 0, t == TP - 1)
                last.then_inc(slab_done, 1)

            for c in range(KD):
                conv_in(c)
                if c >= 1:
                    conv_taps(c - 1)
            conv_taps(KD - 1)
            pe.wait_ge(vsum_step, KD - 1)
            pe.matmul(row, ones[:, :], v_sum[:, :], start=True, stop=True).then_inc(mean_done, 1)
            pe.wait_ge(vc_done, KD)
            stats(2)
            for i in range(4):
                pe.wait_ge(lo_done, N_OUT + i + 1)
                if i >= 2:
                    pe.wait_ge(x_done, KD + 2 * (i - 1))
                two_chunks(i % 2, pair[i % 2], 2 * KD if i == 0 else None).then_inc(slab_done, 1)
                if i >= 1:
                    ada_reduce(Q_OUT + i - 1, ada_acc)
            stats(3)
            ffn(1, 3)
            stats(4)
            ffn(2, 4)
            stats(5)

            def head_sums(c):
                pe.wait_ge(con_s, 48)
                pe.wait_ge(qksq_done, c + 1)
                pe.matmul(ps[0:32, 6 + c // KD, :], ind[:, c % KD, :], sq_tmp[:, c % 2, :], start=(c % KD == 0),
                          stop=(c % KD == KD - 1)).then_inc(ind_done, 1)

            def head_spread(b):
                pe.wait_ge(y_done, 2 * (b // KD) + 2)
                if b >= 2:
                    pe.wait_ge(qkn_done, b - 1)
                w = sel[:, b % KD, :]
                pe.matmul(down_ps[b % 2], w, y_hi[:, :], start=True, stop=False)
                pe.matmul(down_ps[b % 2], w, y_lo[:, :], start=False, stop=True).then_inc(bc_done, 1)

            for s in range(12):
                n = N_QKV + s
                pe.wait_ge(lo_done, n + 1)
                if s < 8:
                    two_chunks(s % 2, pair[s % 2], 5 * KD if s == 0 else None).then_inc(slab_done, 1)
                else:
                    w = wsp[s % 2]
                    for c in range(4):
                        dst = pair[s % 2][c // 2][:, 256 * (c % 2):256 * (c % 2) + 256]
                        for k in range(KD):
                            at = slice(2 * P * k, 2 * P * (k + 1))
                            cols = slice(P * c, P * (c + 1))
                            last = triple(dst, h_hi[:, k, cols], h_lo[:, k, cols], w[:, 0, at], w[:, 1, at],
                                          k == 0, k == KD - 1)
                    last.then_inc(slab_done, 1)
                if 1 <= s <= 8:
                    head_sums(2 * s - 2)
                    head_sums(2 * s - 1)
                if s >= 5:
                    for b in range(2 * (s - 5), 2 * (s - 5) + 2 if s < 11 else 16):
                        head_spread(b)

            at_key = [0, S, 2 * S, 2 * S - P]

            def span(base, c, q0):
                return slice(base + at_key[c] + q0 - P * c, base + at_key[c] + S - P * c)

            def logits(t):
                base = 3 * S * (t % 2)
                c2, half = t // 2, t % 2
                rows = slice(HD * half, HD * half + HD)
                pe.wait_ge(qks_step, 4 * c2 + 4)
                if t >= 2:
                    pe.wait_ge(a_done, t - 1)
                if t == 0:
                    pe.wait_ge(conr_done, 2)
                    pe.wait_ge(vlo_done, 8)
                for c in (0, 1, 3, 2):
                    pe.matmul(zps[:, base + at_key[c]:base + at_key[c] + P], con[:, 0, :], con[:, 1, :],
                              start=(c != 3), stop=False, skip_group_check=True)
                for c in (0, 1, 3, 2):
                    keys = slice(P * c, P * (c + 1))
                    seen = slice(P * c, S)
                    last = triple(zps[:, span(base, c, P * c)], qk_s[rows, c2 % 2, 2, keys],
                                  qk_s[rows, c2 % 2, 3, keys], qk_s[rows, c2 % 2, 0, seen],
                                  qk_s[rows, c2 % 2, 1, seen], False, False)
                last.then_inc(z_done, 1)

            def suffix(t):
                base = 3 * S * (t % 2)
                for part, w in ((sp_hi, sphi_done), (sp_lo, splo_done)):
                    pe.wait_ge(w, t + 1)
                    for c in range(4):
                        for later in range(c, 4):
                            last = pe.matmul(zps[:, span(base, c, P * later)],
                                             con[:, 2 if later == c else 3, :],
                                             part[:, span(0, later, P * later)],
                                             start=False, stop=(part is sp_lo), skip_group_check=True)
                last.then_inc(cum_done, 1)

            def values(t):
                c2 = t // 2
                cols = slice(P * c2, P * (c2 + 1))
                pe.wait_ge(ahi_done, t + 1)
                pe.wait_ge(alo_done, t + 1)
                if t >= 2:
                    pe.wait_ge(o_done, t - 1)
                for c in range(4):
                    last = triple(ps[:, 6 + t % 2, P * c:S], v_hi[:, c, cols], v_lo[:, c, cols],
                                  a_hi[:, span(0, c, P * c)], a_lo[:, span(0, c, P * c)], c == 0, c == 3)
                last.then_inc(av_done, 1)

            logits(0)
            for t in range(HEADS):
                if t + 1 < HEADS:
                    logits(t + 1)
                suffix(t)
                if t >= 1:
                    values(t - 1)
            values(HEADS - 1)
            pe.wait_ge(o_done, HEADS)
            for i in range(4):
                pe.wait_ge(lo_done, N_WO + i + 1)
                if i >= 2:
                    pe.wait_ge(x_done, 4 * KD + 2 * (i - 1))
                two_chunks(i % 2, pair[i % 2]).then_inc(slab_done, 1)
            stats(6)
            ffn(3, 6)


def kernel(**inputs):
    import concourse.bacc as bacc
    from concourse.bass_utils import run_bass_kernel_spmd

    a = {k: np.asarray(v) for k, v in inputs.items()}

    def cols(v):
        return np.ascontiguousarray(v.reshape(-1, P).T)

    def slabs(w, rows, width):
        w = w.reshape(-1, w.shape[-2] // (rows * P), rows, P, w.shape[-1] // width, width)
        return w.transpose(0, 4, 1, 3, 2, 5).reshape(-1, P, rows * width)

    up = np.stack([a["ffn_w1"].reshape(NFFN, KD, P, KF, P), a["ffn_w3"].reshape(NFFN, KD, P, KF, P)], axis=4)
    up = up.transpose(0, 3, 2, 1, 4, 5).reshape(NFFN * KF, P, SLAB)
    down = slabs(a["ffn_w2"].reshape(NFFN, F, D), HF, P)
    w_in = a["a_w_in"][0].reshape(KD, P, 2, KD, P).transpose(3, 1, 0, 2, 4).reshape(KD, P, SLAB)
    mix = np.concatenate([w_in, slabs(a["a_w_out"][0], KD, 2 * P), slabs(a["b_w_qkv"][0], KD, 2 * P),
                          slabs(a["b_w_o"][0], KD, 2 * P)])
    ada = np.concatenate([slabs(a["cond_w"], 4, GW), slabs(a["ada_w"][0], 4, GW), slabs(a["ada_w"][1], 4, GW)])
    head = lambda g: np.concatenate([g, g]).reshape(P, 1)
    vec = np.concatenate([
        cols(a["norm_g"]), cols(a["ada_b"]), cols(a["cond_b"]), cols(a["c"]), cols(a["a_b_in"][0]),
        cols(a["a_dw_b"][0]), cols(a["a_ln_g"][0]), cols(a["a_ln_b"][0]), cols(a["a_b_out"][0]),
        head(a["b_q_g"][0]), head(a["b_k_g"][0])], axis=1)
    dw = a["a_dw"][0].reshape(W, KD, P).transpose(2, 1, 0)
    x_t = a["x"][0].reshape(S, KD, P).transpose(2, 1, 0)
    i = np.arange(P)
    con = np.stack([np.eye(P), np.where(i[:, None] >= i[None, :], NEG, 0.0),
                    np.where(i[:, None] >= i[None, :], -1.0, 0.0), -np.ones((P, P))], axis=1)
    ind = np.zeros((P, KD, 32))
    sel = np.zeros((32, KD, P))
    for c in range(KD):
        for b in range(2):
            ind[HD * b:HD * (b + 1), c, 2 * c + b] = 1.0
            sel[2 * c + b, c, HD * b:HD * (b + 1)] = 1.0

    nc = bacc.Bacc("TRN2", target_bir_lowering=False, num_devices=1)
    arrays, args = {}, []
    for name, v in (("x_t", x_t), ("up", up), ("down", down), ("mix", mix), ("ada", ada), ("vec", vec), ("dw", dw),
                    ("con", con), ("ind", ind), ("sel", sel)):
        v = np.ascontiguousarray(v, dtype=np.float32)
        arrays[name + "_d"] = v
        args.append(nc.dram_tensor(name + "_d", v.shape, F32, kind="ExternalInput").ap())
    out = nc.dram_tensor("out_t", (P, KD, S), F32, kind="ExternalOutput").ap()
    trunk(nc, *args, out)
    r = run_bass_kernel_spmd(nc, [arrays], core_ids=[0])
    got = r.results[0]["out_t"]
    return np.ascontiguousarray(got.transpose(2, 1, 0).reshape(1, S, D))
```

```python
from contextlib import ExitStack

import numpy as np
import concourse.bass as bass
from concourse import mybir

F32 = mybir.dt.float32
F32R = mybir.dt.float32r
ALU = mybir.AluOpType
ACT = mybir.ActivationFunctionType

P = 128
S = 512
D = 1024
F = 2816
KD = D // P
KF = F // P
HF = KF // 2
W = 31
TP = [8] * 7 + [14]
TG = [9] * 7 + [6]
TV = [31 - p - g for p, g in zip(TP, TG)]
NPROD = 8
HEADS = 16
HD = D // HEADS
EPS = 1e-6
EXP_LN_SET = 6
NEG = -1.0e30
SLAB = KD * 2 * P
DOWN = HF * P
GW = 512
NFFN = 4
PIECE = [slice(512, 1280), slice(0, 512)]
QL = S + (S - P) + P + (S - 2 * P)

N_UP = [0, 50, 88, 142]
N_DOWN = [n + KF for n in N_UP]
N_CONV = N_DOWN[0] + 2 * KD
N_OUT = N_CONV + KD
N_QKV = N_DOWN[2] + 2 * KD
N_WO = N_QKV + 12
assert N_UP[1] == N_OUT + 4 and N_UP[2] == N_DOWN[1] + 2 * KD and N_UP[3] == N_WO + 4

VEC = {}
_at = 0
for _name, _n in (("norm_g", 6 * KD), ("ada_b", 2 * 9 * KD), ("cond_b", KD), ("c", KD), ("b_in", 2 * KD),
                  ("dw_b", KD), ("ln_g", KD), ("ln_b", KD), ("b_out", KD), ("qk_g", 2)):
    VEC[_name] = _at
    _at += _n
NVEC = _at

Q_FFN = [6, 20, 31]
Q_BODIES = [11, 11, 7, 0]
Q_DOWN = 17


def trunk(nc, x_in, up_in, down_in, mix_in, ada_in, vec_in, dw_in, con_in, ind_in, sel_in, out):
    ctx = ExitStack()
    with ctx:
        def sb(name, shape, dt=F32):
            return ctx.enter_context(nc.sbuf_tensor(name, shape, dt))

        def sem(name):
            return ctx.enter_context(nc.semaphore(name))

        x = sb("x", [P, KD, S])
        h_hi = sb("h_hi", [P, KD, S], F32R)
        h_lo = sb("h_lo", [P, KD, S], F32R)
        act_tmp = sb("act_tmp", [P, 2, S])
        sq_tmp = sb("sq_tmp", [P, 2, S])
        ss = sb("ss", [P, S])
        ada_acc = sb("ada_acc", [P, GW])
        ident = sb("ident", [P, P])
        ones = sb("ones", [P, P])
        vec = sb("vec", [P, NVEC])
        mods = sb("mods", [P, 2 * 9 * KD])
        e_pre = sb("e_pre", [P, KD])
        e_col = sb("e_col", [P, KD])
        gs = sb("gs", [P, KD])
        gt = sb("gt", [P, KD])
        st = sb("st", [P, 24])
        eps_col = st[:, 22:23]
        raw0 = sb("raw0", [P, SLAB])
        w0 = sb("w0", [P, 2, SLAB], F32R)
        raw = [raw0, None]
        wsp = [w0, None]

        with ExitStack() as scope:
            def ov(name, shape, dt=F32):
                return scope.enter_context(nc.sbuf_tensor(name, shape, dt))
            raw[1] = ov("raw1", [P, SLAB])
            wsp[1] = ov("w1", [P, 2, SLAB], F32R)
            ada_raw = ov("ada_raw", [P, 4, GW])
            g_hi = ov("g_hi", [P, KF, S], F32R)
            g_lo = ov("g_lo", [P, KF, S], F32R)
        with ExitStack() as scope:
            ov("pad_a", [P, 4 * SLAB])
            stage = [ov(f"stage{i}", [P, 4, GW]) for i in range(6)]
        with ExitStack() as scope:
            ov("pad_b", [P, 4 * SLAB])
            v = ov("v", [P, KD, S])
            u = ov("u", [P, 2, S + W - 1])
            u_hi = ov("u_hi", [P, 2, S + W - 1], F32R)
            u_lo = ov("u_lo", [P, 2, S + W - 1], F32R)
            v_odd = ov("v_odd", [P, S])
            v_pool = ov("v_pool", [P, 2, S])
            v_sum = ov("v_sum", [P, S])
            prod = ov("prod", [P, NPROD, S])
            taps_w = ov("taps_w", [P, 2, 2, max(TP) * P], F32R)
            dw = ov("dw", [P, KD, W])
            dw_hi = ov("dw_hi", [P, KD, W], F32R)
            dw_lo = ov("dw_lo", [P, KD, W])
        with ExitStack() as scope:
            sp_abs = ov("sp_abs", [P, 2, QL])
            sp_hi = ov("sp_hi", [P, QL], F32R)
            sp_lo = ov("sp_lo", [P, QL], F32R)
            a_hi = ov("a_hi", [P, QL], F32R)
            a_lo = ov("a_lo", [P, QL], F32R)
            ov("pad_c", [P, S])
            qk = ov("qk", [P, 2 * KD, S])
            v_hi = ov("v_hi", [P, 4, D], F32R)
            v_lo = ov("v_lo", [P, 4, D], F32R)
            qk_s = ov("qk_s", [P, 2, 4, S], F32R)
            con = ov("con", [P, 4, P], F32R)
            a_f = ov("a_f", [P, QL])
        with ExitStack() as scope:
            ov("pad_d", [P, 3 * SLAB])
            sel = ov("sel", [32, KD, P], F32R)
            ov("pad_e", [P, KD * P])
            ov("pad_f", [P, 2 * KD * S + 2 * 4 * D])
            y = ov("y", [32, 4, S])
            y_hi = ov("y_hi", [32, S], F32R)
            y_lo = ov("y_lo", [32, S], F32R)
            sel_f = ov("sel_f", [32, KD, P])
            ov("pad_g", [P, 4 * P])
            con_f = ov("con_f", [P, 4, P])
            ind = ov("ind", [P, KD, 32])

        ps = ctx.enter_context(nc.psum_tensor("ps", [P, 8, S], F32))
        pair = [[ps[:, 0, :], ps[:, 1, :]], [ps[:, 2, :], ps[:, 3, :]]]
        down_ps = [ps[:, 4, :], ps[:, 5, :]]
        row = ps[:, 6, :]
        ada_ps = ps[:, 7, 0:4]
        zps = ps[:, :, :].rearrange("p b s -> p (b s)")

        x_in_s = [sem(f"x_in{i}") for i in range(2)]
        vec_s = sem("vec_in")
        stage_s = [sem(f"stage_in{i}") for i in range(6)]
        raw_s = [sem("raw0_in"), sem("raw1_in")]
        ada_s = sem("ada_in")
        dw_s = sem("dw_in")
        con_s = sem("con_in")
        out_s = sem("out_written")
        ones_done = sem("ones_done")
        hi_done = sem("hi_done")
        lo_done = sem("lo_done")
        slab_done = sem("slab_done")
        ada_step = sem("ada_step")
        start_pe = sem("start_pe")
        ada_sum = sem("ada_sum")
        mod_done = sem("mod_done")
        e_done = sem("e_done")
        sq_done = sem("sq_done")
        ss_step = sem("ss_step")
        lnsq_done = sem("lnsq_done")
        stat_done = sem("stat_done")
        vec_step = sem("vec_step")
        sqrt_done = sem("sqrt_done")
        fac_step = sem("fac_step")
        gs_done = sem("gs_done")
        gate_done = sem("gate_done")
        rdiag_done = sem("rdiag_done")
        row_done = sem("row_done")
        t_done = sem("t_done")
        hhi_done = sem("hhi_done")
        h_done = sem("h_done")
        silu_done = sem("silu_done")
        g_full = sem("g_full")
        ghi_done = sem("ghi_done")
        g_done = sem("g_done")
        x_done = sem("x_done")
        sig_done = sem("sig_done")
        u_done = sem("u_done")
        uhi_done = sem("uhi_done")
        ulo_done = sem("ulo_done")
        tap_step = sem("tap_step")
        vodd_done = sem("vodd_done")
        bo_step = sem("bo_step")
        prod_done = sem("prod_done")
        pool_step = sem("pool_step")
        tapw_done = sem("tapw_done")
        tapp_done = sem("tapp_done")
        dws_done = sem("dws_done")
        comb_step = sem("comb_step")
        v_done = sem("v_done")
        pad_done = sem("pad_done")
        vsum_step = sem("vsum_step")
        mean_done = sem("mean_done")
        vc_done = sem("vc_done")
        yact_done = sem("yact_done")
        conr_done = sem("conr_done")
        qk_done = sem("qk_done")
        qksq_done = sem("qksq_done")
        ind_done = sem("ind_done")
        yv_done = sem("yv_done")
        ysq_done = sem("ysq_done")
        yn_step = sem("yn_step")
        y_done = sem("y_done")
        bc_done = sem("bc_done")
        qkn_done = sem("qkn_done")
        vhi_done = sem("vhi_done")
        vlo_done = sem("vlo_done")
        qks_step = sem("qks_step")
        z_done = sem("z_done")
        ln_step = sem("ln_step")
        sp_done = sem("sp_done")
        sphi_done = sem("sphi_done")
        splo_b_done = sem("splo_b_done")
        splo_a_done = sem("splo_a_done")
        cum_done = sem("cum_done")
        a_done = sem("a_done")
        ahi_done = sem("ahi_done")
        alo_done = sem("alo_done")
        av_done = sem("av_done")
        ohi_done = sem("ohi_done")
        o_done = sem("o_done")

        block = ctx.enter_context(nc.Block())

        def vcol(name, i, n=1):
            return vec[:, VEC[name] + i:VEC[name] + i + n]

        def mod(layer, sub, which, i=0, n=KD):
            at = ((layer * 3 + sub) * 3 + which) * KD + i
            return mods[:, at:at + n]

        def f32(ap):
            return ap.bitcast(F32)

        def z_of(t, p):
            base = 3 * S * (t % 2)
            return zps[:, base + PIECE[p].start:base + PIECE[p].stop]

        def pool_steps(c, j):
            return sum(TG[:c]) - c + max(1, j)

        def ss_steps(m):
            return 6 * (m if m < 3 else m - 1)

        def t_buf(c):
            return (sq_tmp if c % 4 >= 2 else act_tmp)[:, c % 2, :]

        @block.sync
        def _(sp):
            def load(n, src, cols=SLAB):
                if n >= 2:
                    sp.wait_ge(lo_done, n - 1)
                sp.dma_start(raw[n % 2][:, 0:cols], src).then_inc(raw_s[n % 2], 16)

            def load_ada(a):
                sp.wait_ge(ada_step, 4 * a - 24)
                sp.dma_start(ada_raw[:, :, :].rearrange("p k n -> p (k n)"), ada_in[a, :, :]).then_inc(ada_s, 16)

            def up_loads(j, i, ada):
                for s in range(2):
                    sp.wait_ge(lo_done, N_UP[j] + 2 * i + s + 1)
                    sp.dma_start(raw[s][:, :], up_in[KF * j + 2 * i + 2 + s, :, :]).then_inc(raw_s[s], 16)
                    if ada:
                        load_ada(2 * (Q_FFN[j] + i) + s)

            def ffn_loads(j):
                nb = Q_BODIES[j]
                with sp.Fori(0, min(nb, 10)) if nb else ExitStack() as i:
                    if nb:
                        up_loads(j, i, True)
                if nb < 10:
                    with sp.Fori(nb, 10) as i:
                        up_loads(j, i, False)
                for s in range(2):
                    load(N_DOWN[j] + s, down_in[2 * KD * j + s, :, :], DOWN)
                    if nb == 11:
                        load_ada(2 * (Q_FFN[j] + 10) + s)
                for lo_i, hi_i in ((1, 7), (7, KD)) if j == 0 else ((1, KD),):
                    with sp.Fori(lo_i, hi_i) as i:
                        for s in range(2):
                            sp.wait_ge(lo_done, N_DOWN[j] + 2 * i - 1 + s)
                            sp.dma_start(raw[s][:, 0:DOWN], down_in[2 * KD * j + 2 * i + s, :, :]) \
                                .then_inc(raw_s[s], 16)
                        if hi_i == 7:
                            load_ada(2 * Q_DOWN - 1 + i)

            sp.dma_start(vec[:, :], vec_in).then_inc(vec_s, 16)
            sp.dma_start(ident[:, :], con_in[:, 0, :]).then_inc(vec_s, 16)
            for a in range(12):
                if a >= 6 and a % 2 == 0:
                    sp.wait_ge(ada_step, 4 * ((a - 6) // 2 + 1))
                elif a >= 6:
                    sp.wait_ge(start_pe, (a - 7) // 2 + 1)
                sp.dma_start(stage[a % 6][:, :, :].rearrange("p k n -> p (k n)"), ada_in[a, :, :]) \
                    .then_inc(stage_s[a % 6], 16)
                if a == 5:
                    for i in range(2):
                        sp.dma_start(x[:, 4 * i:4 * i + 4, :], x_in[:, 4 * i:4 * i + 4, :]).then_inc(x_in_s[i], 16)
                if a == 9:
                    load(N_UP[0], up_in[0, :, :])
            load(N_UP[0] + 1, up_in[1, :, :])
            ffn_loads(0)
            for c in range(KD):
                load(N_CONV + c, mix_in[c, :, :])
                if c == 1:
                    sp.wait_ge(x_done, KD)
                    sp.dma_start(dw[:, :, :], dw_in).then_inc(dw_s, 16)
            for i in range(4):
                load(N_OUT + i, mix_in[8 + i, :, :])
            for s in range(2):
                load(N_UP[1] + s, up_in[KF + s, :, :])
            ffn_loads(1)
            for s in range(2):
                load(N_UP[2] + s, up_in[2 * KF + s, :, :])
            ffn_loads(2)
            for s in range(12):
                load(N_QKV + s, mix_in[12 + s, :, :])
                if s == 1:
                    sp.wait_ge(x_done, 4 * KD)
                    sp.dma_start(con_f[:, :, :], con_in).then_inc(con_s, 16)
                    sp.dma_start(ind[:, :, :], ind_in).then_inc(con_s, 16)
                    sp.dma_start(sel_f[:, :, :], sel_in).then_inc(con_s, 16)
            load(N_WO, mix_in[24, :, :])
            sp.wait_ge(av_done, HEADS)
            for i in range(1, 4):
                load(N_WO + i, mix_in[24 + i, :, :])
            for s in range(2):
                load(N_UP[3] + s, up_in[3 * KF + s, :, :])
            ffn_loads(3)
            for d in range(KD):
                sp.wait_ge(x_done, 5 * KD + d + 1)
                sp.dma_start(out[:, d, :], x[:, d, :]).then_inc(out_s, 16)
            sp.wait_ge(out_s, 16 * KD)

        @block.gpsimd
        def _(pool):
            pool.memset(eps_col, EPS).then_inc(ones_done, 1)
            pool.memset(ones[:, :], 1.0).then_inc(ones_done, 1)

            def squares(m, c):
                if c == 0 or c == KD - 1:
                    return
                pool.wait_ge(sq_done, KD * m + c + 1)
                if c > 1:
                    pool.wait_ge(ss_step, ss_steps(m) + c - 1)
                a = sq_tmp[:, 0, :] if c == 1 else ss[:, :]
                pool.tensor_tensor(ss[:, :], a, sq_tmp[:, c % 2, :], ALU.add).then_inc(ss_step, 1)

            for c in range(KD):
                squares(0, c)
            for c in range(KD):
                squares(1, c)

            def v_add(c):
                pool.wait_ge(v_done, c + 1)
                if c > 1:
                    pool.wait_ge(vsum_step, c - 1)
                a = v[:, 0, :] if c == 1 else v_sum[:, :]
                pool.tensor_tensor(v_sum[:, :], a, v[:, c, :], ALU.add).then_inc(vsum_step, 1)

            pool.wait_ge(dws_done, 2)
            for c in range(KD):
                if c >= 2:
                    pool.wait_ge(tapp_done, c - 1)
                for part, weight in ((0, f32(dw_hi[:, c, W - TP[c]:])), (1, dw_lo[:, c, W - TP[c]:])):
                    pool.tensor_tensor(
                        taps_w[:, c % 2, part, 0:TP[c] * P].rearrange("p (t m) -> p t m", t=TP[c]),
                        ident[:, :].rearrange("p (t m) -> p t m", t=1).broadcast_to((P, TP[c], P)),
                        weight.rearrange("p (t m) -> p t m", m=1).broadcast_to((P, TP[c], P)),
                        ALU.mult).then_inc(tapw_done, 1)
                if c >= 2:
                    pool.wait_ge(v_done, c - 1)
                for j in range(1, TG[c]):
                    k = sum(TG[:c]) + j
                    pool.wait_ge(prod_done, k + 1)
                    if j > 1:
                        pool.wait_ge(pool_step, pool_steps(c, j - 1))
                    a = prod[:, (k - 1) % NPROD, :] if j == 1 else v_pool[:, c % 2, :]
                    pool.tensor_tensor(v_pool[:, c % 2, :], a, prod[:, k % NPROD, :], ALU.add).then_inc(pool_step, 1)
                if c >= 2:
                    v_add(c - 1)
            for m in range(3, 6):
                for c in range(KD):
                    squares(m, c)

            def sp_low(t):
                pool.wait_ge(sphi_done, 2 * t + 1)
                if t >= 1:
                    pool.wait_ge(cum_done, 2 * t)
                pool.tensor_tensor(sp_lo[:, PIECE[0]], sp_abs[:, t % 2, PIECE[0]], f32(sp_hi[:, PIECE[0]]),
                                   ALU.subtract).then_inc(splo_b_done, 1)

            def a_low(t):
                pool.wait_ge(ahi_done, t + 1)
                if t >= 1:
                    pool.wait_ge(av_done, t)
                pool.tensor_tensor(a_lo[:, :], a_f[:, :], f32(a_hi[:, :]), ALU.subtract).then_inc(alo_done, 1)

            for t in range(HEADS):
                sp_low(t)
                if t >= 1:
                    a_low(t - 1)
            a_low(HEADS - 1)
            for c in range(KD):
                squares(6, c)

        @block.scalar
        def _(act):
            def hi(n, cols=SLAB):
                act.wait_ge(raw_s[n % 2], 16 * (n // 2 + 1))
                if n >= 2:
                    act.wait_ge(slab_done, n - 1)
                act.activation(wsp[n % 2][:, 0, 0:cols], raw[n % 2][:, 0:cols], ACT.Copy).then_inc(hi_done, 1)

            def square(m, c, src, ready, value):
                act.wait_ge(ready, value)
                if c >= 2 and m == 2:
                    act.wait_ge(lnsq_done, c - 1)
                elif c >= 2:
                    act.wait_ge(ss_step, ss_steps(m) + max(1, c - 2))
                act.activation(sq_tmp[:, c % 2, :], src, ACT.Square).then_inc(sq_done, 1)

            def table():
                act.wait_ge(ones_done, 2)
                act.activation(st[:, 20:21], ones[:, 0:1], ACT.Sqrt)

            def root(m):
                act.wait_ge(stat_done, m + 1)
                act.activation(st[:, 4:8], row[:, 0:4], ACT.Sqrt, bias=eps_col, scale=1.0 / D) \
                    .then_inc(sqrt_done, 1)

            def h_his(m, layer, sub):
                for c in range(KD):
                    act.wait_ge(t_done, KD * m + c + 1)
                    act.activation(h_hi[:, c, :], t_buf(c), ACT.Identity,
                                   bias=mod(layer, sub, 0, c, 1)).then_inc(hhi_done, 1)

            def up_step(j, i, s, split=True):
                n = N_UP[j] + 2 * i + s
                act.wait_ge(slab_done, n + 1)
                act.activation(act_tmp[:, s, :], pair[s][0], ACT.Silu).then_inc(silu_done, 1)
                act.wait_ge(g_full, KF * j + 2 * i + s + 1)
                act.activation(g_hi[:, 2 * i + s, :], act_tmp[:, s, :], ACT.Copy).then_inc(ghi_done, 1)
                if split:
                    act.wait_ge(raw_s[s], 16 * (N_UP[j] // 2 + 2) + 16 * i)
                    act.activation(wsp[s][:, 0, :], raw[s][:, :], ACT.Copy).then_inc(hi_done, 1)

            def ffn(j, m, nxt, last=False):
                with act.Fori(0, 10) as i:
                    for s in range(2):
                        up_step(j, i, s)
                for s in range(2):
                    up_step(j, 10, s, split=False)
                    hi(N_DOWN[j] + s, DOWN)
                if not last:
                    table()
                for d in range(KD):
                    if d < KD - 1:
                        hi(N_DOWN[j] + 2 * d + 2, DOWN)
                        hi(N_DOWN[j] + 2 * d + 3, DOWN)
                    elif not last:
                        hi(nxt)
                    if not last:
                        square(m, d, x[:, d, :], x_done, KD * max(0, m - 2) + d + 1)
                if not last:
                    hi(nxt + 1)

            act.wait_ge(ones_done, 2)
            act.activation(st[:, 21:22], ones[:, 0:1], ACT.Silu)
            act.wait_ge(mod_done, 2)
            act.activation(e_col[:, :], e_pre[:, :], ACT.Silu).then_inc(e_done, 1)
            for c in range(KD):
                square(0, c, x[:, c, :], x_in_s[c // 4], 16)
            table()
            root(0)
            hi(N_UP[0])
            hi(N_UP[0] + 1)
            h_his(0, 0, 0)
            ffn(0, 1, N_CONV)
            root(1)
            h_his(1, 0, 1)

            for c in range(KD):
                act.wait_ge(slab_done, N_CONV + c + 1)
                act.activation(act_tmp[:, c % 2, :], pair[c % 2][1], ACT.Sigmoid, bias=vcol("b_in", KD + c)) \
                    .then_inc(sig_done, 1)
                act.wait_ge(u_done, c + 1)
                act.activation(u_hi[:, c % 2, W - 1:], u[:, c % 2, W - 1:], ACT.Copy).then_inc(uhi_done, 1)
                if c == 0:
                    act.wait_ge(pad_done, 3)
                if c < KD - 1:
                    hi(N_CONV + c + 2)
                for j in range(TG[c]):
                    k, t = sum(TG[:c]) + j, TV[c] + j
                    if k >= NPROD:
                        before = k - NPROD
                        b = max(i for i in range(KD) if sum(TG[:i]) <= before)
                        act.wait_ge(pool_step, pool_steps(b, before - sum(TG[:b])))
                    act.activation(prod[:, k % NPROD, :], u[:, c % 2, t:t + S], ACT.Copy, scale=dw[:, c, t:t + 1]) \
                        .then_inc(prod_done, 1)
            hi(N_OUT + 1)
            for c in range(KD):
                square(2, c, v[:, c, :], vc_done, c + 1)
            table()
            root(2)
            for c in range(KD):
                act.wait_ge(t_done, KD * 2 + c + 1)
                act.activation(t_buf(c), t_buf(c), ACT.Silu, scale=vcol("ln_g", c),
                               bias=vcol("ln_b", c)).then_inc(yact_done, 1)
                act.wait_ge(yact_done, c + 1)
                act.activation(h_hi[:, c, :], t_buf(c), ACT.Copy).then_inc(hhi_done, 1)

            def out_steps(n0, m, nxt):
                for i in range(4):
                    if i < 2:
                        hi(n0 + i + 2)
                    elif i == 2:
                        hi(nxt)
                    for d in (2 * i, 2 * i + 1):
                        square(m, d, x[:, d, :], x_done, KD * (m - 2) + d + 1)
                hi(nxt + 1)

            table()
            out_steps(N_OUT, 3, N_UP[1])
            root(3)
            h_his(3, 0, 2)
            ffn(1, 4, N_UP[2])
            root(4)
            h_his(4, 1, 0)
            ffn(2, 5, N_QKV)
            root(5)
            h_his(5, 1, 1)

            def y_root(g):
                act.wait_ge(yv_done, g + 1)
                act.activation(y[:, 1, :], y[:, 0, :], ACT.Sqrt).then_inc(ysq_done, 1)

            for s in range(12):
                if s < 11:
                    hi(N_QKV + s + 2)
                if s < 8:
                    for c in (2 * s, 2 * s + 1):
                        act.wait_ge(qk_done, c + 1)
                        if c >= 2:
                            act.wait_ge(ind_done, c - 1)
                        act.activation(sq_tmp[:, c % 2, :], qk[:, c, :], ACT.Square).then_inc(qksq_done, 1)
                else:
                    act.wait_ge(slab_done, N_QKV + s + 1)
                    for b in range(2):
                        act.activation(v_hi[:, 2 * b:2 * b + 2, 256 * (s - 8):256 * (s - 7)],
                                       pair[s % 2][b].rearrange("p (c n) -> p c n", c=2), ACT.Copy) \
                            .then_inc(vhi_done, 1)
                if s == 4:
                    y_root(0)
                if s == 8:
                    y_root(1)

            def o_high(t):
                act.wait_ge(av_done, t + 1)
                q = slice(HD * (t % 2), HD * (t % 2) + HD)
                act.activation(h_hi[q, t // 2, :], ps[q, 6 + t % 2, :], ACT.Copy).then_inc(ohi_done, 1)

            def weights(t):
                for p in range(2):
                    act.wait_ge(cum_done, 2 * t + p + 1)
                    if t >= 1 and p == 0:
                        act.wait_ge(ahi_done, t)
                        act.wait_ge(alo_done, t)
                    act.activation(a_f[:, PIECE[p]], z_of(t, p), ACT.Exp).then_inc(a_done, 1)

            act.add_instruction(mybir.InstLoadActFuncSet(
                name=nc.get_next_instruction_name(), engine=mybir.EngineType.Activation, act_func_set_id=EXP_LN_SET))
            for t in range(HEADS):
                if t == 0:
                    act.wait_ge(slab_done, N_QKV + 12)
                for p in range(2):
                    w = sp_abs[:, t % 2, PIECE[p]]
                    act.wait_ge(z_done, 2 * t + p + 1)
                    if t >= 2:
                        act.wait_ge((splo_b_done, splo_a_done)[p], t - 1)
                    act.activation(w, z_of(t, p), ACT.Abs).then_inc(ln_step, 1)
                    act.wait_ge(ln_step, 6 * t + 3 * p + 1)
                    act.activation(w, w, ACT.Exp, scale=-1.0).then_inc(ln_step, 1)
                    act.wait_ge(ln_step, 6 * t + 3 * p + 2)
                    act.activation(w, w, ACT.Ln, bias=ones[:, 0:1]).then_inc(ln_step, 1)
                if t >= 1:
                    weights(t - 1)
                if t >= 2:
                    o_high(t - 2)
            weights(HEADS - 1)
            o_high(HEADS - 2)
            o_high(HEADS - 1)
            hi(N_WO + 1)
            table()
            out_steps(N_WO, 6, N_UP[3])
            root(6)
            h_his(6, 1, 2)
            ffn(3, None, None, last=True)

        @block.vector
        def _(dve):
            def lo(n, cols=SLAB):
                dve.wait_ge(hi_done, n + 1)
                dve.tensor_tensor(wsp[n % 2][:, 1, 0:cols], raw[n % 2][:, 0:cols], f32(wsp[n % 2][:, 0, 0:cols]), ALU.subtract) \
                    .then_inc(lo_done, 1)

            def ada_half(q, s, buf, acc):
                for k in range(4):
                    a = (4 * q if isinstance(q, int) and q < 6 else 8 * q - 24 + 4 * s) + k
                    col = 4 * s + k
                    w = e_col[:, col:col + 1] if not isinstance(q, int) or q >= 2 else vcol("c", col)
                    if s == 0 and k == 0:
                        dve.tensor_scalar(acc, buf[:, k, :], w, None, ALU.mult).then_inc(ada_step, 1)
                    else:
                        dve.wait_ge(ada_step, a)
                        dve.scalar_tensor_tensor(out=acc, in0=buf[:, k, :], scalar=w, in1=acc, op0=ALU.mult,
                                                 op1=ALU.add).then_inc(ada_step, 1)

            def ada_take(q):
                dve.wait_ge(ada_sum, q + 1)
                if isinstance(q, int) and q < 2:
                    dst, b = e_pre[:, 4 * q:4 * q + 4], vcol("cond_b", 4 * q, 4)
                else:
                    dst = mods[:, :].rearrange("p (g n) -> p g n", n=4)[:, q - 2, :]
                    b = vcol("ada_b", 0, 144).rearrange("p (g n) -> p g n", n=4)[:, q - 2, :]
                dve.tensor_tensor(dst, ada_ps, b, ALU.add).then_inc(mod_done, 1)

            def factor(m):
                vv, sd, y0, y1 = st[:, 0:4], st[:, 4:8], st[:, 8:12], st[:, 16:20]
                dve.wait_ge(sqrt_done, m + 1)
                dve.tensor_scalar(vv, row[:, 0:4], 1.0 / D, EPS, ALU.mult, ALU.add).then_inc(vec_step, 1)
                dve.reciprocal(y0, sd).then_inc(vec_step, 1)
                dve.wait_ge(vec_step, 4 * m + 2)
                dve.tensor_tensor(y1, y0, y0, ALU.mult).then_inc(vec_step, 1)
                dve.wait_ge(vec_step, 4 * m + 3)
                dve.scalar_tensor_tensor(out=y1, in0=y1, scalar=-0.5, in1=vv, op0=ALU.mult, op1=ALU.mult) \
                    .then_inc(vec_step, 1)
                dve.wait_ge(vec_step, 4 * m + 4)
                dve.scalar_tensor_tensor(out=sd, in0=y1, scalar=1.5, in1=y0, op0=ALU.add, op1=ALU.mult) \
                    .then_inc(fac_step, 1)
                dve.wait_ge(fac_step, m + 1)
                dve.tensor_tensor(
                    sq_tmp[:, 0, :].rearrange("p (c m) -> p c m", c=4),
                    ident[:, :].rearrange("p (c m) -> p c m", c=1).broadcast_to((P, 4, P)),
                    sd.rearrange("p (c m) -> p c m", m=1).broadcast_to((P, 4, P)),
                    ALU.mult).then_inc(rdiag_done, 1)

            def h_lows(m, layer, sub):
                dve.wait_ge(mod_done, 2 + 18 * layer + 6 * sub + 4)
                dve.scalar_tensor_tensor(out=gs[:, :], in0=mod(layer, sub, 1), scalar=1.0,
                                         in1=vcol("norm_g", (3 * layer + sub) * KD, KD), op0=ALU.add,
                                         op1=ALU.mult).then_inc(gs_done, 1)
                if m:
                    factor(m)
                dve.wait_ge(gs_done, (m if m < 2 else m - 1) + 1)
                dve.wait_ge(row_done, m + 1)
                for c in range(KD + 1):
                    if c < KD:
                        if c >= 4:
                            dve.wait_ge(h_done, KD * m + c - 3)
                        dve.scalar_tensor_tensor(out=t_buf(c), in0=x[:, c, :], scalar=gs[:, c:c + 1],
                                                 in1=row, op0=ALU.mult, op1=ALU.mult).then_inc(t_done, 1)
                    if c >= 1:
                        b = c - 1
                        dve.wait_ge(hhi_done, KD * m + b + 1)
                        dve.scalar_tensor_tensor(out=h_lo[:, b, :], in0=t_buf(b),
                                                 scalar=mod(layer, sub, 0, b, 1), in1=f32(h_hi[:, b, :]),
                                                 op0=ALU.add, op1=ALU.subtract).then_inc(h_done, 1)

            def gate(layer, sub, k, factor_):
                dve.wait_ge(mod_done, 2 + 18 * layer + 6 * sub + 6)
                dve.tensor_scalar(gt[:, :], mod(layer, sub, 2), 1.0, factor_, ALU.add, ALU.mult).then_inc(gate_done, 1)
                dve.wait_ge(gate_done, k)

            def x_add(d, src):
                dve.scalar_tensor_tensor(out=x[:, d, :], in0=src, scalar=gt[:, d:d + 1], in1=x[:, d, :],
                                         op0=ALU.mult, op1=ALU.add).then_inc(x_done, 1)

            def up_step(j, i, s, ada, split=True, take=True):
                n = N_UP[j] + 2 * i + s
                f = KF * j + 2 * i + s
                dve.wait_ge(silu_done, f + 1)
                dve.tensor_tensor(act_tmp[:, s, :], act_tmp[:, s, :], pair[s][1], ALU.mult).then_inc(g_full, 1)
                dve.wait_ge(ghi_done, f + 1)
                dve.tensor_tensor(g_lo[:, 2 * i + s, :], act_tmp[:, s, :], f32(g_hi[:, 2 * i + s, :]),
                                  ALU.subtract).then_inc(g_done, 1)
                if split:
                    dve.wait_ge(hi_done, n + 3)
                    dve.tensor_tensor(wsp[s][:, 1, :], raw[s][:, :], f32(wsp[s][:, 0, :]), ALU.subtract) \
                        .then_inc(lo_done, 1)
                else:
                    lo(N_DOWN[j] + s, DOWN)
                if ada:
                    q = Q_FFN[j] + i
                    if s == 0 and take:
                        ada_take(q - 1)
                    dve.wait_ge(ada_s, 16 * (2 * q - 11 + s))
                    ada_half(q, s, ada_raw, ada_acc[:, :])

            def ffn(j, k, layer, sub, nxt, last=False):
                nb = Q_BODIES[j]
                if nb:
                    for s in range(2):
                        up_step(j, 0, s, True, take=False)
                    with dve.Fori(1, min(nb, 10)) as i:
                        for s in range(2):
                            up_step(j, i, s, True)
                if nb < 10:
                    with dve.Fori(nb, 10) as i:
                        for s in range(2):
                            up_step(j, i, s, False)
                    if nb:
                        ada_take(Q_FFN[j] + nb - 1)
                for s in range(2):
                    up_step(j, 10, s, nb == 11, split=False)
                gate(layer, sub, k, 0.5)
                for d in range(KD):
                    if d < KD - 1:
                        lo(N_DOWN[j] + 2 * d + 2, DOWN)
                    elif not last:
                        lo(nxt)
                    dve.wait_ge(slab_done, N_DOWN[j] + 2 * d + 2)
                    x_add(d, down_ps[d % 2])
                    if d < KD - 1:
                        lo(N_DOWN[j] + 2 * d + 3, DOWN)
                    if j == 0 and 1 <= d <= 6:
                        q, s = Q_DOWN + (d - 1) // 2, (d - 1) % 2
                        if s == 0:
                            ada_take(q - 1)
                        dve.wait_ge(ada_s, 16 * (2 * q - 11 + s))
                        ada_half(q, s, ada_raw, ada_acc[:, :])
                if nb == 11:
                    ada_take(Q_FFN[j] + 10 if j else Q_DOWN + 2)

            dve.wait_ge(vec_s, 32)
            for q in range(6):
                if q == 2:
                    ada_take(1)
                    dve.wait_ge(e_done, 1)
                dve.wait_ge(stage_s[2 * q % 6], 16 * (q // 3 + 1))
                ada_half(q, 0, stage[2 * q % 6], act_tmp[:, q % 2, :])
                if q >= 1 and q != 2:
                    ada_take(q - 1)
                if q == 4:
                    factor(0)
            lo(N_UP[0])
            ada_take(5)
            h_lows(0, 0, 0)
            lo(N_UP[0] + 1)
            ffn(0, 1, 0, 0, N_CONV)
            h_lows(1, 0, 1)
            lo(N_CONV + 1)

            dve.wait_ge(dw_s, 16)
            dve.tensor_copy(dw_hi[:, :, :], dw[:, :, :]).then_inc(dws_done, 1)
            dve.wait_ge(dws_done, 1)
            dve.tensor_tensor(dw_lo[:, :, :], dw[:, :, :], f32(dw_hi[:, :, :]), ALU.subtract).then_inc(dws_done, 1)
            for b in range(2):
                dve.memset(u[:, b, 0:W - 1], 0.0)
                dve.memset(f32(u_hi[:, b, 0:W - 1]), 0.0)
                last = dve.memset(f32(u_lo[:, b, 0:W - 1]), 0.0)
                last.then_inc(pad_done, 1)
            dve.drain().then_inc(pad_done, 1)
            dve.wait_ge(pad_done, 3)

            def taps(c, lo_t, hi_t):
                before = sum(TV[:c])
                for t in range(lo_t, hi_t):
                    src = u[:, c % 2, t:t + S]
                    w = dw[:, c, t:t + 1]
                    dst = v[:, c, :] if t % 2 == 0 else v_odd[:, :]
                    if t == 0:
                        ins = dve.tensor_scalar(dst, src, w, vcol("dw_b", c), ALU.mult, ALU.add)
                    elif t == 1:
                        if c >= 1:
                            dve.wait_ge(vodd_done, c)
                        ins = dve.tensor_scalar(dst, src, w, None, ALU.mult)
                    else:
                        dve.wait_ge(tap_step, before + t - 1)
                        ins = dve.scalar_tensor_tensor(out=dst, in0=src, scalar=w, in1=dst, op0=ALU.mult, op1=ALU.add)
                    ins.then_inc(tap_step, 1)

            def combine(c):
                dve.wait_ge(tapp_done, c + 1)
                dve.wait_ge(vodd_done, c + 1)
                dve.tensor_tensor(v[:, c, :], v[:, c, :], down_ps[c % 2], ALU.add).then_inc(comb_step, 1)
                dve.wait_ge(comb_step, c + 1)
                dve.wait_ge(pool_step, pool_steps(c, TG[c] - 1))
                dve.tensor_tensor(v[:, c, :], v[:, c, :], v_pool[:, c % 2, :], ALU.add).then_inc(v_done, 1)

            for c in range(KD):
                dve.wait_ge(sig_done, c + 1)
                dve.scalar_tensor_tensor(out=u[:, c % 2, W - 1:], in0=pair[c % 2][0], scalar=vcol("b_in", c),
                                         in1=act_tmp[:, c % 2, :], op0=ALU.add, op1=ALU.mult).then_inc(u_done, 1)
                dve.wait_ge(uhi_done, c + 1)
                dve.tensor_tensor(u_lo[:, c % 2, W - 1:], u[:, c % 2, W - 1:], f32(u_hi[:, c % 2, W - 1:]),
                                  ALU.subtract).then_inc(ulo_done, 1)
                taps(c, 0, 4)
                if c < KD - 1:
                    lo(N_CONV + c + 2)
                taps(c, 4, 6)
                if c >= 1:
                    combine(c - 1)
                taps(c, 6, TV[c])
                dve.wait_ge(tap_step, sum(TV[:c + 1]))
                dve.tensor_tensor(v[:, c, :], v[:, c, :], v_odd[:, :], ALU.add).then_inc(vodd_done, 1)
            combine(KD - 1)
            dve.wait_ge(mean_done, 1)
            for c in range(KD):
                dve.scalar_tensor_tensor(out=v[:, c, :], in0=row, scalar=-1.0 / D, in1=v[:, c, :], op0=ALU.mult,
                                         op1=ALU.add).then_inc(vc_done, 1)
            lo(N_OUT + 1)
            factor(2)
            dve.wait_ge(row_done, 3)
            for c in range(KD + 1):
                if c < KD:
                    if c >= 4:
                        dve.wait_ge(h_done, KD * 2 + c - 3)
                    dve.tensor_tensor(t_buf(c), v[:, c, :], row, ALU.mult).then_inc(t_done, 1)
                if c >= 1:
                    b = c - 1
                    dve.wait_ge(hhi_done, KD * 2 + b + 1)
                    dve.tensor_tensor(h_lo[:, b, :], t_buf(b), f32(h_hi[:, b, :]), ALU.subtract) \
                        .then_inc(h_done, 1)
            gate(0, 1, 2, 1.0)
            for i in range(4):
                if i < 2:
                    lo(N_OUT + i + 2)
                elif i == 2:
                    lo(N_UP[1])
                dve.wait_ge(slab_done, N_OUT + i + 1)
                if i >= 1:
                    dve.wait_ge(x_done, KD + 2 * i)
                for b in range(2):
                    d = 2 * i + b
                    dve.tensor_scalar(act_tmp[:, b, :], pair[i % 2][b], vcol("b_out", d), gt[:, d:d + 1], ALU.add,
                                      ALU.mult).then_inc(bo_step, 1)
                for b in range(2):
                    d = 2 * i + b
                    dve.wait_ge(bo_step, d + 1)
                    dve.tensor_tensor(x[:, d, :], x[:, d, :], act_tmp[:, b, :], ALU.add).then_inc(x_done, 1)
            h_lows(3, 0, 2)
            lo(N_UP[1] + 1)
            ffn(1, 3, 0, 2, N_UP[2])
            h_lows(4, 1, 0)
            lo(N_UP[2] + 1)
            ffn(2, 4, 1, 0, N_QKV)
            h_lows(5, 1, 1)
            lo(N_QKV + 1)

            dve.wait_ge(con_s, 48)
            dve.tensor_copy(con[:, :, :], con_f[:, :, :]).then_inc(conr_done, 1)
            dve.tensor_copy(sel[:, :, :], sel_f[:, :, :]).then_inc(conr_done, 1)

            def head_factors(g):
                dve.wait_ge(ind_done, KD * (g + 1))
                dve.tensor_scalar(y[:, 0, :], ps[0:32, 6 + g, :], 1.0 / HD, EPS, ALU.mult, ALU.add).then_inc(yv_done, 1)
                dve.wait_ge(ysq_done, g + 1)
                dve.reciprocal(y[:, 2, :], y[:, 1, :]).then_inc(yn_step, 1)
                dve.wait_ge(yn_step, 4 * g + 1)
                dve.tensor_tensor(y[:, 3, :], y[:, 2, :], y[:, 2, :], ALU.mult).then_inc(yn_step, 1)
                dve.wait_ge(yn_step, 4 * g + 2)
                dve.scalar_tensor_tensor(out=y[:, 3, :], in0=y[:, 3, :], scalar=-0.5, in1=y[:, 0, :], op0=ALU.mult,
                                         op1=ALU.mult).then_inc(yn_step, 1)
                dve.wait_ge(yn_step, 4 * g + 3)
                dve.scalar_tensor_tensor(out=y[:, 3, :], in0=y[:, 3, :], scalar=1.5, in1=y[:, 2, :], op0=ALU.add,
                                         op1=ALU.mult).then_inc(yn_step, 1)
                dve.wait_ge(yn_step, 4 * g + 4)
                if g == 1:
                    dve.wait_ge(bc_done, KD)
                dve.tensor_copy(y_hi[:, :], y[:, 3, :]).then_inc(y_done, 1)
                dve.wait_ge(y_done, 2 * g + 1)
                dve.tensor_tensor(y_lo[:, :], y[:, 3, :], f32(y_hi[:, :]), ALU.subtract).then_inc(y_done, 1)

            def normalise(b):
                dve.wait_ge(bc_done, b + 1)
                dve.scalar_tensor_tensor(out=qk[:, b, :], in0=qk[:, b, :], scalar=vcol("qk_g", b // KD),
                                         in1=down_ps[b % 2], op0=ALU.mult, op1=ALU.mult).then_inc(qkn_done, 1)

            for s in range(12):
                n = N_QKV + s
                dve.wait_ge(slab_done, n + 1)
                if s < 8:
                    for b in range(2):
                        dve.tensor_copy(qk[:, 2 * s + b, :], pair[s % 2][b]).then_inc(qk_done, 1)
                else:
                    for b in range(2):
                        dve.wait_ge(vhi_done, 2 * (s - 8) + b + 1)
                        at = (slice(None), slice(2 * b, 2 * b + 2), slice(256 * (s - 8), 256 * (s - 7)))
                        dve.tensor_tensor(v_lo[at], pair[s % 2][b].rearrange("p (c n) -> p c n", c=2),
                                          f32(v_hi[at]), ALU.subtract).then_inc(vlo_done, 1)
                if s < 11:
                    lo(n + 2)
                if s == 4:
                    head_factors(0)
                if s == 8:
                    normalise(6)
                    normalise(7)
                    head_factors(1)
                elif s >= 5:
                    for b in range(2 * (s - 5), 2 * (s - 5) + 2 if s < 11 else 16):
                        normalise(b)

            def split_qk(c):
                b = c % 2
                if c >= 2:
                    dve.wait_ge(z_done, 4 * c - 4)
                if c == 0:
                    dve.wait_ge(qkn_done, 16)
                dve.tensor_scalar(qk_s[:, b, 0, :], qk[:, c, :], HD ** -0.5, None, ALU.mult).then_inc(qks_step, 1)
                dve.tensor_copy(qk_s[:, b, 2, :], qk[:, KD + c, :]).then_inc(qks_step, 1)
                dve.wait_ge(qks_step, 4 * c + 1)
                dve.scalar_tensor_tensor(out=qk_s[:, b, 1, :], in0=qk[:, c, :], scalar=HD ** -0.5,
                                         in1=f32(qk_s[:, b, 0, :]), op0=ALU.mult, op1=ALU.subtract) \
                    .then_inc(qks_step, 1)
                dve.wait_ge(qks_step, 4 * c + 2)
                dve.tensor_tensor(qk_s[:, b, 3, :], qk[:, KD + c, :], f32(qk_s[:, b, 2, :]), ALU.subtract) \
                    .then_inc(qks_step, 1)

            def softplus(t, p):
                w = sp_abs[:, t % 2, PIECE[p]]
                dve.wait_ge(ln_step, 6 * t + 3 * p + 3)
                dve.scalar_tensor_tensor(out=w, in0=z_of(t, p), scalar=0.0, in1=w, op0=ALU.max, op1=ALU.add) \
                    .then_inc(sp_done, 1)
                dve.wait_ge(sp_done, 2 * t + p + 1)
                if t >= 1:
                    dve.wait_ge(cum_done, 2 * t)
                dve.tensor_copy(sp_hi[:, PIECE[p]], w).then_inc(sphi_done, 1)
                if p == 1:
                    dve.wait_ge(sphi_done, 2 * t + 2)
                    dve.tensor_tensor(sp_lo[:, PIECE[1]], w, f32(sp_hi[:, PIECE[1]]), ALU.subtract) \
                        .then_inc(splo_a_done, 1)

            def a_high(t):
                dve.wait_ge(a_done, 2 * t + 2)
                if t >= 1:
                    dve.wait_ge(av_done, t)
                dve.tensor_copy(a_hi[:, :], a_f[:, :]).then_inc(ahi_done, 1)

            def o_low(t):
                q = slice(HD * (t % 2), HD * (t % 2) + HD)
                dve.wait_ge(ohi_done, t + 1)
                dve.tensor_tensor(h_lo[q, t // 2, :], ps[q, 6 + t % 2, :], f32(h_hi[q, t // 2, :]), ALU.subtract) \
                    .then_inc(o_done, 1)

            split_qk(0)
            for t in range(HEADS):
                softplus(t, 0)
                softplus(t, 1)
                if t >= 1:
                    a_high(t - 1)
                if t >= 2:
                    o_low(t - 2)
                if t % 2 == 0 and t // 2 + 1 < KD:
                    split_qk(t // 2 + 1)
            a_high(HEADS - 1)
            o_low(HEADS - 2)
            o_low(HEADS - 1)
            gate(1, 1, 5, 1.0)
            lo(N_WO + 1)
            for i in range(4):
                if i < 2:
                    lo(N_WO + i + 2)
                elif i == 2:
                    lo(N_UP[3])
                dve.wait_ge(slab_done, N_WO + i + 1)
                for b in range(2):
                    x_add(2 * i + b, pair[i % 2][b])
            h_lows(6, 1, 2)
            lo(N_UP[3] + 1)
            ffn(3, 6, 1, 2, None, last=True)

        @block.tensor
        def _(pe):
            def triple(dst, a_hi_, a_lo_, b_hi_, b_lo_, start, stop):
                pe.matmul(dst, a_hi_, b_hi_, start=start, stop=False, skip_group_check=True)
                pe.matmul(dst, a_hi_, b_lo_, start=False, stop=False, skip_group_check=True)
                return pe.matmul(dst, a_lo_, b_hi_, start=False, stop=stop, skip_group_check=True)

            def two_chunks(slot, banks, k0=None):
                w = wsp[slot]
                for k in range(KD):
                    if k0 is not None:
                        pe.wait_ge(h_done, k0 + k + 1)
                    for b in range(2):
                        at = slice((2 * k + b) * P, (2 * k + b + 1) * P)
                        last = triple(banks[b], w[:, 0, at], w[:, 1, at], h_hi[:, k, :], h_lo[:, k, :],
                                      k == 0, k == KD - 1)
                return last

            def stats(m):
                def add(src, first, sem_):
                    for c in range(4):
                        last = pe.matmul(row[:, c:c + 1], src[:, c * P:(c + 1) * P], ones[:, 0:1],
                                         start=(first and c == 0), stop=(not first), skip_group_check=True)
                    if sem_ is not None:
                        last.then_inc(sem_, 1)

                if m == 2:
                    for c in range(KD):
                        pe.wait_ge(sq_done, KD * m + c + 1)
                        add(sq_tmp[:, c % 2, :], c == 0, lnsq_done if c < KD - 1 else stat_done)
                else:
                    pe.wait_ge(ss_step, ss_steps(m) + 6)
                    add(ss, True, None)
                    pe.wait_ge(sq_done, KD * m + KD)
                    add(sq_tmp[:, 1, :], False, stat_done)
                pe.wait_ge(rdiag_done, m + 1)
                pe.matmul(row, ones[:, :], sq_tmp[:, 0, :], start=True, stop=True).then_inc(row_done, 1)

            def ada_reduce(q, acc):
                pe.wait_ge(ada_step, 8 * q - 16)
                for c in range(4):
                    last = pe.matmul(ada_ps[:, c:c + 1], acc[:, c * P:(c + 1) * P], ones[:, 0:1], start=True, stop=True)
                last.then_inc(ada_sum, 1)

            def start_group(q):
                if q == 2:
                    pe.wait_ge(e_done, 1)
                pe.wait_ge(stage_s[(2 * q + 1) % 6], 16 * (q // 3 + 1))
                if q >= 1:
                    pe.wait_ge(mod_done, q)
                w = stage[(2 * q + 1) % 6]
                for c in range(4):
                    for k in range(4):
                        b = e_col[:, 4 + k:5 + k] if q >= 2 else vcol("c", 4 + k)
                        last = pe.matmul(ada_ps[:, c:c + 1], w[:, k, c * P:(c + 1) * P], b,
                                         start=(c == 0 and k == 0), stop=False, skip_group_check=True)
                last.then_inc(start_pe, 1)
                pe.wait_ge(ada_step, 4 * q + 4)
                for c in range(4):
                    last = pe.matmul(ada_ps[:, c:c + 1], act_tmp[:, q % 2, c * P:(c + 1) * P], ones[:, 0:1],
                                     start=False, stop=True, skip_group_check=True)
                last.then_inc(ada_sum, 1)

            def up_step(j, i, s, m, ada):
                pe.wait_ge(lo_done, N_UP[j] + 2 * i + s + 1)
                two_chunks(s, pair[s], m if m is None else KD * m).then_inc(slab_done, 1)
                if ada and s == 0:
                    ada_reduce(Q_FFN[j] + i - 1, ada_acc)

            def ffn(j, m):
                nb = Q_BODIES[j]
                up_step(j, 0, 0, m, False)
                up_step(j, 0, 1, None, False)
                if nb:
                    with pe.Fori(1, min(nb + 1, 11)) as i:
                        for s in range(2):
                            up_step(j, i, s, None, True)
                if nb < 11:
                    with pe.Fori(nb + 1, 11) as i:
                        for s in range(2):
                            up_step(j, i, s, None, False)
                with pe.Fori(0, KD // 2) as i:
                    for s in range(2):
                        for half in range(2):
                            pe.wait_ge(lo_done, N_DOWN[j] + 4 * i + 2 * s + half + 1)
                            pe.wait_ge(g_done, KF * j + HF * (half + 1))
                            w = wsp[half]
                            for k in range(HF):
                                at = slice(k * P, (k + 1) * P)
                                f = HF * half + k
                                last = triple(down_ps[s], w[:, 0, at], w[:, 1, at], g_hi[:, f, :], g_lo[:, f, :],
                                              f == 0, f == KF - 1)
                            last.then_inc(slab_done, 1)
                    if j == 0:
                        ada_reduce(Q_DOWN - 1 + i, ada_acc)
                if j and nb == 11:
                    ada_reduce(Q_FFN[j] + 10, ada_acc)

            pe.wait_ge(ones_done, 2)
            pe.wait_ge(vec_s, 32)
            for q in range(5):
                start_group(q)
            stats(0)
            start_group(5)
            ffn(0, 0)
            stats(1)

            def conv_in(c):
                pe.wait_ge(lo_done, N_CONV + c + 1)
                if c >= 2:
                    pe.wait_ge(u_done, c - 1)
                two_chunks(c % 2, pair[c % 2], KD if c == 0 else None).then_inc(slab_done, 1)

            def conv_taps(c):
                pe.wait_ge(tapw_done, 2 * c + 2)
                pe.wait_ge(ulo_done, c + 1)
                if c >= 2:
                    pe.wait_ge(v_done, c - 1)
                w = taps_w[:, c % 2, :, :]
                for t in range(TP[c]):
                    at = slice(t * P, (t + 1) * P)
                    u0 = W - TP[c] + t
                    last = triple(down_ps[c % 2], w[:, 0, at], w[:, 1, at], u_hi[:, c % 2, u0:u0 + S],
                                  u_lo[:, c % 2, u0:u0 + S], t == 0, t == TP[c] - 1)
                last.then_inc(tapp_done, 1)

            for c in range(KD):
                conv_in(c)
                if c >= 1:
                    conv_taps(c - 1)
            conv_taps(KD - 1)
            pe.wait_ge(vsum_step, KD - 2)
            pe.matmul(row, ones[:, :], v_sum[:, :], start=True, stop=False)
            pe.wait_ge(v_done, KD)
            pe.matmul(row, ones[:, :], v[:, KD - 1, :], start=False, stop=True).then_inc(mean_done, 1)
            pe.wait_ge(vc_done, KD)
            stats(2)
            for i in range(4):
                pe.wait_ge(lo_done, N_OUT + i + 1)
                if i >= 2:
                    pe.wait_ge(x_done, KD + 2 * (i - 1))
                two_chunks(i % 2, pair[i % 2], 2 * KD if i == 0 else None).then_inc(slab_done, 1)
            stats(3)
            ffn(1, 3)
            stats(4)
            ffn(2, 4)
            stats(5)

            def head_sums(c):
                pe.wait_ge(con_s, 48)
                pe.wait_ge(qksq_done, c + 1)
                pe.matmul(ps[0:32, 6 + c // KD, :], ind[:, c % KD, :], sq_tmp[:, c % 2, :], start=(c % KD == 0),
                          stop=(c % KD == KD - 1)).then_inc(ind_done, 1)

            def head_spread(b):
                pe.wait_ge(y_done, 2 * (b // KD) + 2)
                if b >= 2:
                    pe.wait_ge(qkn_done, b - 1)
                w = sel[:, b % KD, :]
                pe.matmul(down_ps[b % 2], w, y_hi[:, :], start=True, stop=False)
                pe.matmul(down_ps[b % 2], w, y_lo[:, :], start=False, stop=True).then_inc(bc_done, 1)

            for s in range(12):
                n = N_QKV + s
                pe.wait_ge(lo_done, n + 1)
                if s < 8:
                    two_chunks(s % 2, pair[s % 2], 5 * KD if s == 0 else None).then_inc(slab_done, 1)
                else:
                    w = wsp[s % 2]
                    for c in range(4):
                        dst = pair[s % 2][c // 2][:, 256 * (c % 2):256 * (c % 2) + 256]
                        for k in range(KD):
                            at = slice(2 * P * k, 2 * P * (k + 1))
                            cols = slice(P * c, P * (c + 1))
                            last = triple(dst, h_hi[:, k, cols], h_lo[:, k, cols], w[:, 0, at], w[:, 1, at],
                                          k == 0, k == KD - 1)
                    last.then_inc(slab_done, 1)
                if 1 <= s <= 8:
                    head_sums(2 * s - 2)
                    head_sums(2 * s - 1)
                if s >= 5:
                    for b in range(2 * (s - 5), 2 * (s - 5) + 2 if s < 11 else 16):
                        head_spread(b)

            at_key = [0, S, 2 * S, 2 * S - P]

            def span(base, c, q0):
                return slice(base + at_key[c] + q0 - P * c, base + at_key[c] + S - P * c)

            def logits(t):
                base = 3 * S * (t % 2)
                c2, half = t // 2, t % 2
                rows = slice(HD * half, HD * half + HD)
                pe.wait_ge(qks_step, 4 * c2 + 4)
                if t == 0:
                    pe.wait_ge(conr_done, 2)
                    pe.wait_ge(vlo_done, 8)
                for p, blocks in enumerate(((1, 3, 2), (0,))):
                    if t >= 2:
                        pe.wait_ge(a_done, 2 * (t - 2) + p + 1)
                    for c in blocks:
                        pe.matmul(zps[:, base + at_key[c]:base + at_key[c] + P], con[:, 0, :], con[:, 1, :],
                                  start=(c != 3), stop=False, skip_group_check=True)
                    for c in blocks:
                        keys = slice(P * c, P * (c + 1))
                        seen = slice(P * c, S)
                        last = triple(zps[:, span(base, c, P * c)], qk_s[rows, c2 % 2, 2, keys],
                                      qk_s[rows, c2 % 2, 3, keys], qk_s[rows, c2 % 2, 0, seen],
                                      qk_s[rows, c2 % 2, 1, seen], False, False)
                    last.then_inc(z_done, 1)

            def suffix(t):
                base = 3 * S * (t % 2)
                for p, blocks in enumerate(((1, 2, 3), (0,))):
                    for part in (sp_hi, sp_lo):
                        if part is sp_hi:
                            pe.wait_ge(sphi_done, 2 * t + p + 1)
                        else:
                            pe.wait_ge((splo_b_done, splo_a_done)[p], t + 1)
                        for c in blocks:
                            for later in range(c, 4):
                                last = pe.matmul(zps[:, span(base, c, P * later)],
                                                 con[:, 2 if later == c else 3, :],
                                                 part[:, span(0, later, P * later)],
                                                 start=False, stop=(part is sp_lo), skip_group_check=True)
                    last.then_inc(cum_done, 1)

            def values(t):
                c2 = t // 2
                cols = slice(P * c2, P * (c2 + 1))
                pe.wait_ge(ahi_done, t + 1)
                pe.wait_ge(alo_done, t + 1)
                if t >= 2:
                    pe.wait_ge(o_done, t - 1)
                for c in range(4):
                    last = triple(ps[:, 6 + t % 2, P * c:S], v_hi[:, c, cols], v_lo[:, c, cols],
                                  a_hi[:, span(0, c, P * c)], a_lo[:, span(0, c, P * c)], c == 0, c == 3)
                last.then_inc(av_done, 1)

            logits(0)
            for t in range(HEADS):
                if t + 1 < HEADS:
                    logits(t + 1)
                suffix(t)
                if t >= 1:
                    values(t - 1)
            values(HEADS - 1)
            pe.wait_ge(o_done, HEADS)
            for i in range(4):
                pe.wait_ge(lo_done, N_WO + i + 1)
                if i >= 2:
                    pe.wait_ge(x_done, 4 * KD + 2 * (i - 1))
                two_chunks(i % 2, pair[i % 2]).then_inc(slab_done, 1)
            stats(6)
            ffn(3, 6)


def kernel(**inputs):
    import concourse.bacc as bacc
    from concourse.bass_utils import run_bass_kernel_spmd

    a = {k: np.asarray(v) for k, v in inputs.items()}

    def cols(v):
        return np.ascontiguousarray(v.reshape(-1, P).T)

    def slabs(w, rows, width):
        w = w.reshape(-1, w.shape[-2] // (rows * P), rows, P, w.shape[-1] // width, width)
        return w.transpose(0, 4, 1, 3, 2, 5).reshape(-1, P, rows * width)

    up = np.stack([a["ffn_w1"].reshape(NFFN, KD, P, KF, P), a["ffn_w3"].reshape(NFFN, KD, P, KF, P)], axis=4)
    up = up.transpose(0, 3, 2, 1, 4, 5).reshape(NFFN * KF, P, SLAB)
    down = slabs(a["ffn_w2"].reshape(NFFN, F, D), HF, P)
    w_in = a["a_w_in"][0].reshape(KD, P, 2, KD, P).transpose(3, 1, 0, 2, 4).reshape(KD, P, SLAB)
    mix = np.concatenate([w_in, slabs(a["a_w_out"][0], KD, 2 * P), slabs(a["b_w_qkv"][0], KD, 2 * P),
                          slabs(a["b_w_o"][0], KD, 2 * P)])
    ada = np.concatenate([slabs(a["cond_w"], 4, GW), slabs(a["ada_w"][0], 4, GW), slabs(a["ada_w"][1], 4, GW)])
    head = lambda g: np.concatenate([g, g]).reshape(P, 1)
    vec = np.concatenate([
        cols(a["norm_g"]), cols(a["ada_b"]), cols(a["cond_b"]), cols(a["c"]), cols(a["a_b_in"][0]),
        cols(a["a_dw_b"][0]), cols(a["a_ln_g"][0]), cols(a["a_ln_b"][0]), cols(a["a_b_out"][0]),
        head(a["b_q_g"][0]), head(a["b_k_g"][0])], axis=1)
    dw = a["a_dw"][0].reshape(W, KD, P).transpose(2, 1, 0)
    x_t = a["x"][0].reshape(S, KD, P).transpose(2, 1, 0)
    i = np.arange(P)
    con = np.stack([np.eye(P), np.where(i[:, None] >= i[None, :], NEG, 0.0),
                    np.where(i[:, None] >= i[None, :], -1.0, 0.0), -np.ones((P, P))], axis=1)
    ind = np.zeros((P, KD, 32))
    sel = np.zeros((32, KD, P))
    for c in range(KD):
        for b in range(2):
            ind[HD * b:HD * (b + 1), c, 2 * c + b] = 1.0
            sel[2 * c + b, c, HD * b:HD * (b + 1)] = 1.0

    nc = bacc.Bacc("TRN2", target_bir_lowering=False, num_devices=1)
    arrays, args = {}, []
    for name, v in (("x_t", x_t), ("up", up), ("down", down), ("mix", mix), ("ada", ada), ("vec", vec), ("dw", dw),
                    ("con", con), ("ind", ind), ("sel", sel)):
        v = np.ascontiguousarray(v, dtype=np.float32)
        arrays[name + "_d"] = v
        args.append(nc.dram_tensor(name + "_d", v.shape, F32, kind="ExternalInput").ap())
    out = nc.dram_tensor("out_t", (P, KD, S), F32, kind="ExternalOutput").ap()
    trunk(nc, *args, out)
    r = run_bass_kernel_spmd(nc, [arrays], core_ids=[0])
    got = r.results[0]["out_t"]
    return np.ascontiguousarray(got.transpose(2, 1, 0).reshape(1, S, D))
```

```python
from contextlib import ExitStack

import numpy as np
import concourse.bass as bass
from concourse import mybir

F32 = mybir.dt.float32
F32R = mybir.dt.float32r
ALU = mybir.AluOpType
ACT = mybir.ActivationFunctionType

P = 128
S = 512
D = 1024
F = 2816
KD = D // P
KF = F // P
HF = KF // 2
W = 31
TP = [8] * 6 + [11, 16]
TG = [9] * 6 + [6, 3]
TV = [31 - p - g for p, g in zip(TP, TG)]
NPROD = 8
HEADS = 16
HD = D // HEADS
EPS = 1e-6
EXP_LN_SET = 6
NEG = -1.0e30
SLAB = KD * 2 * P
DOWN = HF * P
GW = 512
NFFN = 4
PIECE = [slice(512, 1280), slice(0, 512)]
QL = S + (S - P) + P + (S - 2 * P)

N_UP = [0, 50, 88, 142]
N_DOWN = [n + KF for n in N_UP]
N_CONV = N_DOWN[0] + 2 * KD
N_OUT = N_CONV + KD
N_QKV = N_DOWN[2] + 2 * KD
N_WO = N_QKV + 12
assert N_UP[1] == N_OUT + 4 and N_UP[2] == N_DOWN[1] + 2 * KD and N_UP[3] == N_WO + 4

VEC = {}
_at = 0
for _name, _n in (("norm_g", 6 * KD), ("ada_b", 2 * 9 * KD), ("cond_b", KD), ("c", KD), ("b_in", 2 * KD),
                  ("dw_b", KD), ("ln_g", KD), ("ln_b", KD), ("b_out", KD), ("qk_g", 2)):
    VEC[_name] = _at
    _at += _n
NVEC = _at

START_ROWS = [6, 6, 6, 7, 7, 7]
STEP0 = sum(START_ROWS)
Q_FFN = [6, 20, 31]
Q_BODIES = [11, 11, 7, 0]
N_SPLIT = [0, 10, 20]
Q_DOWN = 17


def trunk(nc, x_in, up_in, down_in, mix_in, ada_in, vec_in, dw_in, con_in, ind_in, sel_in, out):
    ctx = ExitStack()
    with ctx:
        def sb(name, shape, dt=F32):
            return ctx.enter_context(nc.sbuf_tensor(name, shape, dt))

        def sem(name):
            return ctx.enter_context(nc.semaphore(name))

        x = sb("x", [P, KD, S])
        h_hi = sb("h_hi", [P, KD, S], F32R)
        h_lo = sb("h_lo", [P, KD, S], F32R)
        act_tmp = sb("act_tmp", [P, 2, S])
        with nc.sbuf_tensor("sq_tmp", [P, 2, S], F32) as sq_tmp:
            pass
        parts = sb("parts", [P, 2, S], F32R)
        ss = sb("ss", [P, S])
        ada_acc = sb("ada_acc", [P, GW])
        acc_hi, acc_lo = parts[:, 0, :], parts[:, 1, :]
        fac_hi, fac_lo = parts[:, 0, :], parts[:, 1, :]
        ident = sb("ident", [P, P])
        ones = sb("ones", [P, P])
        ones_r = sb("ones_r", [P, P], F32R)
        st_r = sb("st_r", [P, 4], F32R)
        vec = sb("vec", [P, NVEC])
        mods = sb("mods", [P, 2 * 9 * KD])
        e_pre = sb("e_pre", [P, KD])
        e_col = sb("e_col", [P, KD])
        gs = sb("gs", [P, KD])
        gb = sb("gb", [P, KD])
        gt = sb("gt", [P, KD])
        st = sb("st", [P, 24])
        eps_col = st[:, 22:23]
        raw0 = sb("raw0", [P, SLAB])
        w0 = sb("w0", [P, 2, SLAB], F32R)
        raw = [raw0, None]
        wsp = [w0, None]

        with ExitStack() as scope:
            def ov(name, shape, dt=F32):
                return scope.enter_context(nc.sbuf_tensor(name, shape, dt))
            raw[1] = ov("raw1", [P, SLAB])
            wsp[1] = ov("w1", [P, 2, SLAB], F32R)
            ada_raw = ov("ada_raw", [P, 4, GW])
            g_hi = ov("g_hi", [P, KF, S], F32R)
            g_lo = ov("g_lo", [P, KF, S], F32R)
        with ExitStack() as scope:
            ov("pad_a", [P, 4 * SLAB])
            stage = [ov(f"stage{i}", [P, 4, GW]) for i in range(6)]
        with ExitStack() as scope:
            ov("pad_b", [P, 4 * SLAB])
            v = ov("v", [P, KD, S])
            u = ov("u", [P, 2, S + W - 1])
            u_hi = ov("u_hi", [P, 2, S + W - 1], F32R)
            u_lo = ov("u_lo", [P, 2, S + W - 1], F32R)
            v_odd = ov("v_odd", [P, S])
            v_pool = ov("v_pool", [P, 2, S])
            v_sum = ov("v_sum", [P, S])
            prod = ov("prod", [P, NPROD, S])
            taps_w = ov("taps_w", [P, 2, 2, max(TP) * P], F32R)
            dw = ov("dw", [P, KD, W])
            dw_hi = ov("dw_hi", [P, KD, W], F32R)
            dw_lo = ov("dw_lo", [P, KD, W])
        with ExitStack() as scope:
            qk_s = ov("qk_s", [P, 2, 4, S], F32R)
            sp_hi = ov("sp_hi", [P, QL], F32R)
            ov("pad_c", [P, 3 * SLAB - 2 * 4 * S - QL])
            sp_abs = ov("sp_abs", [P, 2, QL])
            sp_lo = ov("sp_lo", [P, QL], F32R)
            a_hi = ov("a_hi", [P, QL], F32R)
            a_lo = ov("a_lo", [P, QL], F32R)
            a_f = ov("a_f", [P, QL])
            qk = ov("qk", [P, 2 * KD, S])
            v_hi = ov("v_hi", [P, 4, D], F32R)
            v_lo = ov("v_lo", [P, 4, D], F32R)
            con = ov("con", [P, 4, P], F32R)
        with ExitStack() as scope:
            ov("pad_d", [P, 3 * SLAB])
            sel = ov("sel", [32, KD, P], F32R)
            y = ov("y", [32, 4, S])
            y_hi = ov("y_hi", [32, S], F32R)
            y_lo = ov("y_lo", [32, S], F32R)
            sel_f = ov("sel_f", [32, KD, P])
            con_f = ov("con_f", [P, 4, P])
            ind = ov("ind", [P, KD, 32])

        ps = ctx.enter_context(nc.psum_tensor("ps", [P, 8, S], F32))
        pair = [[ps[:, 0, :], ps[:, 1, :]], [ps[:, 2, :], ps[:, 3, :]]]
        down_ps = [ps[:, 4, :], ps[:, 5, :]]
        row = ps[:, 6, :]
        ada_ps = ps[:, 7, 0:8]
        mean_row = ps[:, 7, :]
        zps = ps[:, :, :].rearrange("p b s -> p (b s)")

        x_in_s = [sem(f"x_in{i}") for i in range(2)]
        vec_s = sem("vec_in")
        stage_s = [sem(f"stage_in{i}") for i in range(6)]
        raw_s = [sem("raw0_in"), sem("raw1_in")]
        ada_s = sem("ada_in")
        dw_s = sem("dw_in")
        con_s = sem("con_in")
        out_s = sem("out_written")
        ones_done = sem("ones_done")
        hi_done = sem("hi_done")
        lo_done = sem("lo_done")
        slab_done = sem("slab_done")
        half_done = sem("half_done")
        ada_step = sem("ada_step")
        start_pe = sem("start_pe")
        acch_done = sem("acch_done")
        accl_done = sem("accl_done")
        ada_sum = sem("ada_sum")
        mod_done = sem("mod_done")
        e_done = sem("e_done")
        sq_done = sem("sq_done")
        ss_step = sem("ss_step")
        lns_step = sem("lns_step")
        stat_done = sem("stat_done")
        vec_step = sem("vec_step")
        sqrt_done = sem("sqrt_done")
        fac_step = sem("fac_step")
        facr_step = sem("facr_step")
        gs_done = sem("gs_done")
        gate_done = sem("gate_done")
        rdiag_done = sem("rdiag_done")
        row_done = sem("row_done")
        t_done = sem("t_done")
        hhi_done = sem("hhi_done")
        hsum_done = sem("hsum_done")
        h_done = sem("h_done")
        h_odd_done = sem("h_odd_done")
        silu_done = sem("silu_done")
        g_full = sem("g_full")
        ghi_done = sem("ghi_done")
        g_done = sem("g_done")
        x_done = sem("x_done")
        sig_done = sem("sig_done")
        u_done = sem("u_done")
        uhi_done = sem("uhi_done")
        ulo_done = sem("ulo_done")
        tap_step = sem("tap_step")
        vodd_done = sem("vodd_done")
        gb_done = sem("gb_done")
        bo_step = sem("bo_step")
        prod_done = sem("prod_done")
        pool_step = sem("pool_step")
        tapw_done = sem("tapw_done")
        tapp_done = sem("tapp_done")
        dws_done = sem("dws_done")
        comb_step = sem("comb_step")
        v_done = sem("v_done")
        pad_done = sem("pad_done")
        vsum_step = sem("vsum_step")
        mean_done = sem("mean_done")
        vc_done = sem("vc_done")
        yact_done = sem("yact_done")
        conr_done = sem("conr_done")
        qk_done = sem("qk_done")
        qksq_done = sem("qksq_done")
        ind_done = sem("ind_done")
        yv_done = sem("yv_done")
        ysq_done = sem("ysq_done")
        yn_step = sem("yn_step")
        y_done = sem("y_done")
        bc_done = sem("bc_done")
        qkn_done = sem("qkn_done")
        vhi_done = sem("vhi_done")
        vlo_done = sem("vlo_done")
        qks_step = sem("qks_step")
        z_done = sem("z_done")
        ln_step = sem("ln_step")
        sp_done = sem("sp_done")
        sphi_done = sem("sphi_done")
        splo_b_done = sem("splo_b_done")
        splo_a_done = sem("splo_a_done")
        cum_done = sem("cum_done")
        a_done = sem("a_done")
        ahi_done = sem("ahi_done")
        alo_done = sem("alo_done")
        av_done = sem("av_done")
        ohi_done = sem("ohi_done")
        o_done = sem("o_done")

        block = ctx.enter_context(nc.Block())

        def vcol(name, i, n=1):
            return vec[:, VEC[name] + i:VEC[name] + i + n]

        def mod(layer, sub, which, i=0, n=KD):
            at = ((layer * 3 + sub) * 3 + which) * KD + i
            return mods[:, at:at + n]

        def f32(ap):
            return ap.bitcast(F32)

        def z_of(t, p):
            base = 3 * S * (t % 2)
            return zps[:, base + PIECE[p].start:base + PIECE[p].stop]

        def spread_bank(b):
            return down_ps[b % 2] if b < KD or b >= 14 else ps[:, 6 + b % 2, :]

        def pool_steps(c, j):
            return sum(TG[:c]) - c + max(1, j)

        def h_parts(m):
            return 4 * m + (4 if m > 2 else 0)

        def h_odd_parts(m):
            return 4 * m - (4 if m > 2 else 0)

        def ss_steps(m):
            return 6 * m - (3 if m > 2 else 0)

        def t_buf(c):
            return (sq_tmp if c % 4 >= 2 else act_tmp)[:, c % 2, :]

        @block.sync
        def _(sp):
            def load(n, src, cols=SLAB):
                if n >= 2:
                    sp.wait_ge(lo_done, n - 1)
                sp.dma_start(raw[n % 2][:, 0:cols], src).then_inc(raw_s[n % 2], 16)

            def load_ada(a):
                sp.wait_ge(ada_step, 4 * a + (STEP0 - 48))
                sp.dma_start(ada_raw[:, :, :].rearrange("p k n -> p (k n)"), ada_in[a, :, :]).then_inc(ada_s, 16)

            def up_loads(j, i, ada):
                for s in range(2):
                    sp.wait_ge(lo_done, N_UP[j] + 2 * i + s + 1)
                    sp.dma_start(raw[s][:, :], up_in[KF * j + 2 * i + 2 + s, :, :]).then_inc(raw_s[s], 16)
                    if ada:
                        load_ada(2 * (Q_FFN[j] + i) + s)

            def ffn_loads(j):
                nb = Q_BODIES[j]
                with sp.Fori(0, min(nb, 10)) if nb else ExitStack() as i:
                    if nb:
                        up_loads(j, i, True)
                if nb < 10:
                    with sp.Fori(nb, 10) as i:
                        up_loads(j, i, False)
                for s in range(2):
                    load(N_DOWN[j] + s, down_in[2 * KD * j + s, :, :], DOWN)
                    if nb == 11:
                        load_ada(2 * (Q_FFN[j] + 10) + s)
                for lo_i, hi_i in ((1, 7), (7, KD)) if j == 0 else ((1, KD),):
                    with sp.Fori(lo_i, hi_i) as i:
                        for s in range(2):
                            sp.wait_ge(lo_done, N_DOWN[j] + 2 * i - 1 + s)
                            sp.dma_start(raw[s][:, 0:DOWN], down_in[2 * KD * j + 2 * i + s, :, :]) \
                                .then_inc(raw_s[s], 16)
                        if hi_i == 7:
                            load_ada(2 * Q_DOWN - 1 + i)

            sp.dma_start(vec[:, :], vec_in).then_inc(vec_s, 16)
            sp.dma_start(ident[:, :], con_in[:, 0, :]).then_inc(vec_s, 16)
            for a in range(12):
                g = a // 2 - 3
                if a >= 6:
                    sp.wait_ge(ada_step, sum(START_ROWS[:g]) + (START_ROWS[g] if a % 2 else 4))
                if a >= 6 and a % 2:
                    sp.wait_ge(start_pe, g + 1)
                sp.dma_start(stage[a % 6][:, :, :].rearrange("p k n -> p (k n)"), ada_in[a, :, :]) \
                    .then_inc(stage_s[a % 6], 16)
                if a == 5:
                    for i in range(2):
                        sp.dma_start(x[:, 4 * i:4 * i + 4, :], x_in[:, 4 * i:4 * i + 4, :]).then_inc(x_in_s[i], 16)
            for s in range(2):
                load(N_UP[0] + s, up_in[s, :, :])
            ffn_loads(0)
            for c in range(KD):
                load(N_CONV + c, mix_in[c, :, :])
                if c == 1:
                    sp.wait_ge(x_done, KD)
                    sp.dma_start(dw[:, :, :], dw_in).then_inc(dw_s, 16)
            for i in range(4):
                load(N_OUT + i, mix_in[8 + i, :, :])
            for s in range(2):
                load(N_UP[1] + s, up_in[KF + s, :, :])
            ffn_loads(1)
            for s in range(2):
                load(N_UP[2] + s, up_in[2 * KF + s, :, :])
            ffn_loads(2)
            for s in range(12):
                load(N_QKV + s, mix_in[12 + s, :, :])
                if s == 1:
                    sp.wait_ge(x_done, 4 * KD)
                    sp.dma_start(con_f[:, :, :], con_in).then_inc(con_s, 16)
                    sp.dma_start(ind[:, :, :], ind_in).then_inc(con_s, 16)
                    sp.dma_start(sel_f[:, :, :], sel_in).then_inc(con_s, 16)
            load(N_WO, mix_in[24, :, :])
            sp.wait_ge(cum_done, 2 * HEADS)
            for i in range(1, 4):
                load(N_WO + i, mix_in[24 + i, :, :])
            for s in range(2):
                load(N_UP[3] + s, up_in[3 * KF + s, :, :])
            ffn_loads(3)
            for d in range(KD):
                sp.wait_ge(x_done, 5 * KD + d + 1)
                sp.dma_start(out[:, d, :], x[:, d, :]).then_inc(out_s, 16)
            sp.wait_ge(out_s, 16 * KD)

        @block.gpsimd
        def _(pool):
            pool.memset(eps_col, EPS).then_inc(ones_done, 1)
            pool.memset(ones[:, :], 1.0).then_inc(ones_done, 1)

            def squares(m, c):
                if c == 0 or c == KD - 1:
                    return
                pool.wait_ge(sq_done, KD * m + c + 1)
                if c > 1:
                    pool.wait_ge(ss_step, ss_steps(m) + c - 1)
                a = sq_tmp[:, 0, :] if c == 1 else ss[:, :]
                pool.tensor_tensor(ss[:, :], a, sq_tmp[:, c % 2, :], ALU.add).then_inc(ss_step, 1)

            def h_odds(m):
                for c in range(1, KD, 2):
                    pool.wait_ge(hhi_done, KD * m + c + 1)
                    pool.tensor_tensor(h_lo[:, c, :], t_buf(c), f32(h_hi[:, c, :]), ALU.subtract) \
                        .then_inc(h_odd_done, 1)

            def acc_lows(j, n):
                with pool.Fori(0, n) as i:
                    pool.wait_ge(acch_done, i + (N_SPLIT[j] + 1))
                    pool.tensor_tensor(acc_lo, ada_acc[:, :], f32(acc_hi), ALU.subtract).then_inc(accl_done, 1)

            for c in range(KD):
                squares(0, c)
            h_odds(0)
            acc_lows(0, 10)
            for c in range(KD):
                squares(1, c)
            h_odds(1)

            def v_add(c):
                pool.wait_ge(v_done, c + 1)
                if c > 1:
                    pool.wait_ge(vsum_step, c - 1)
                a = v[:, 0, :] if c == 1 else v_sum[:, :]
                pool.tensor_tensor(v_sum[:, :], a, v[:, c, :], ALU.add).then_inc(vsum_step, 1)

            pool.wait_ge(dws_done, 2)
            def tap_matrices(c):
                if c >= 2:
                    pool.wait_ge(tapp_done, c - 1)
                for part, weight in ((0, f32(dw_hi[:, c, W - TP[c]:])), (1, dw_lo[:, c, W - TP[c]:])):
                    pool.tensor_tensor(
                        taps_w[:, c % 2, part, 0:TP[c] * P].rearrange("p (t m) -> p t m", t=TP[c]),
                        ident[:, :].rearrange("p (t m) -> p t m", t=1).broadcast_to((P, TP[c], P)),
                        weight.rearrange("p (t m) -> p t m", m=1).broadcast_to((P, TP[c], P)),
                        ALU.mult).then_inc(tapw_done, 1)

            for c in range(KD):
                if c < KD - 1:
                    tap_matrices(c)
                if c == KD - 2:
                    tap_matrices(KD - 1)
                if c >= 2:
                    pool.wait_ge(v_done, c - 1)
                for j in range(1, TG[c]):
                    k = sum(TG[:c]) + j
                    pool.wait_ge(prod_done, k + 1)
                    if j > 1:
                        pool.wait_ge(pool_step, pool_steps(c, j - 1))
                    a = prod[:, (k - 1) % NPROD, :] if j == 1 else v_pool[:, c % 2, :]
                    pool.tensor_tensor(v_pool[:, c % 2, :], a, prod[:, k % NPROD, :], ALU.add).then_inc(pool_step, 1)
                if c >= 2:
                    v_add(c - 1)
            for c in range(1, 4):
                pool.wait_ge(sq_done, KD * 2 + c + 1)
                if c > 1:
                    pool.wait_ge(ss_step, ss_steps(2) + c - 1)
                a = prod[:, 0, :] if c == 1 else ss[:, :]
                pool.tensor_tensor(ss[:, :], a, prod[:, c, :], ALU.add).then_inc(ss_step, 1)
            for m in range(3, 6):
                for c in range(KD):
                    squares(m, c)
                h_odds(m)
                if m < 5:
                    acc_lows(m - 2, min(Q_BODIES[m - 2], 10))

            def sp_low(t):
                pool.wait_ge(sphi_done, 2 * t + 1)
                if t >= 1:
                    pool.wait_ge(cum_done, 2 * t)
                pool.tensor_tensor(sp_lo[:, PIECE[0]], sp_abs[:, t % 2, PIECE[0]], f32(sp_hi[:, PIECE[0]]),
                                   ALU.subtract).then_inc(splo_b_done, 1)

            def a_low(t):
                pool.wait_ge(ahi_done, t + 1)
                if t >= 1:
                    pool.wait_ge(av_done, t)
                pool.tensor_tensor(a_lo[:, :], a_f[:, :], f32(a_hi[:, :]), ALU.subtract).then_inc(alo_done, 1)

            for t in range(HEADS):
                sp_low(t)
                if t >= 1:
                    a_low(t - 1)
            a_low(HEADS - 1)
            for c in range(KD):
                squares(6, c)
            h_odds(6)

        @block.scalar
        def _(act):
            def hi(n, cols=SLAB):
                act.wait_ge(raw_s[n % 2], 16 * (n // 2 + 1))
                if n >= 2:
                    act.wait_ge(slab_done, n - 1)
                act.activation(wsp[n % 2][:, 0, 0:cols], raw[n % 2][:, 0:cols], ACT.Copy).then_inc(hi_done, 1)

            def square(m, c, src, ready, value):
                act.wait_ge(ready, value)
                if m == 2:
                    act.activation(prod[:, c, :], src, ACT.Square).then_inc(sq_done, 1)
                    return
                if c >= 2:
                    act.wait_ge(ss_step, ss_steps(m) + max(1, c - 2))
                act.activation(sq_tmp[:, c % 2, :], src, ACT.Square).then_inc(sq_done, 1)

            def table():
                act.wait_ge(ones_done, 2)
                act.activation(st[:, 20:21], ones[:, 0:1], ACT.Sqrt)

            def root(m):
                act.wait_ge(stat_done, m + 1)
                act.activation(st[:, 4:8], row[:, 0:4], ACT.Sqrt, bias=eps_col, scale=1.0 / D) \
                    .then_inc(sqrt_done, 1)

            def h_his(m, layer, sub):
                for c in range(KD):
                    act.wait_ge(t_done, KD * m + c + 1)
                    shift = mod(layer, sub, 0, c, 1)
                    if c % 2:
                        act.activation(t_buf(c), t_buf(c), ACT.Identity, bias=shift).then_inc(hsum_done, 1)
                        act.wait_ge(hsum_done, h_odd_parts(m) + c // 2 + 1)
                        act.activation(h_hi[:, c, :], t_buf(c), ACT.Copy).then_inc(hhi_done, 1)
                    else:
                        act.activation(h_hi[:, c, :], t_buf(c), ACT.Identity, bias=shift).then_inc(hhi_done, 1)

            def up_step(j, i, s, split=True, ada=False):
                n = N_UP[j] + 2 * i + s
                if ada and s == 0:
                    act.wait_ge(ada_step, 8 * (Q_FFN[j] + i) + (STEP0 - 48))
                    act.activation(acc_hi, ada_acc[:, :], ACT.Copy).then_inc(acch_done, 1)
                act.wait_ge(slab_done, n + 1)
                act.activation(act_tmp[:, s, :], pair[s][0], ACT.Silu).then_inc(silu_done, 1)
                act.wait_ge(g_full, KF * j + 2 * i + s + 1)
                act.activation(g_hi[:, 2 * i + s, :], act_tmp[:, s, :], ACT.Copy).then_inc(ghi_done, 1)
                if split:
                    act.wait_ge(raw_s[s], 16 * (N_UP[j] // 2 + 2) + 16 * i)
                    act.activation(wsp[s][:, 0, :], raw[s][:, :], ACT.Copy).then_inc(hi_done, 1)

            def ffn(j, m, nxt, last=False):
                nb = Q_BODIES[j]
                for s in range(2):
                    up_step(j, 0, s)
                if nb:
                    with act.Fori(1, min(nb + 1, 10)) as i:
                        for s in range(2):
                            up_step(j, i, s, ada=True)
                if nb < 10:
                    with act.Fori(nb + 1, 10) as i:
                        for s in range(2):
                            up_step(j, i, s)
                for s in range(2):
                    up_step(j, 10, s, split=False, ada=(nb == 11))
                    hi(N_DOWN[j] + s, DOWN)
                if not last:
                    table()
                for d in range(KD):
                    if d < KD - 1:
                        hi(N_DOWN[j] + 2 * d + 2, DOWN)
                        hi(N_DOWN[j] + 2 * d + 3, DOWN)
                    elif not last:
                        hi(nxt)
                    if not last:
                        square(m, d, x[:, d, :], x_done, KD * max(0, m - 2) + d + 1)
                if not last:
                    hi(nxt + 1)

            act.wait_ge(ones_done, 2)
            act.activation(st[:, 21:22], ones[:, 0:1], ACT.Silu)
            act.wait_ge(mod_done, 2)
            act.activation(e_col[:, :], e_pre[:, :], ACT.Silu).then_inc(e_done, 1)
            for c in range(KD):
                square(0, c, x[:, c, :], x_in_s[c // 4], 16)
            table()
            root(0)
            hi(N_UP[0])
            hi(N_UP[0] + 1)
            h_his(0, 0, 0)
            ffn(0, 1, N_CONV)
            root(1)
            h_his(1, 0, 1)

            for c in range(KD):
                act.wait_ge(slab_done, N_CONV + c + 1)
                act.activation(act_tmp[:, c % 2, :], pair[c % 2][1], ACT.Sigmoid, bias=vcol("b_in", KD + c)) \
                    .then_inc(sig_done, 1)
                act.wait_ge(u_done, c + 1)
                act.activation(u_hi[:, c % 2, W - 1:], u[:, c % 2, W - 1:], ACT.Copy).then_inc(uhi_done, 1)
                if c == 0:
                    act.wait_ge(pad_done, 3)
                if c < KD - 1:
                    hi(N_CONV + c + 2)
                for j in range(TG[c]):
                    k, t = sum(TG[:c]) + j, TV[c] + j
                    if k >= NPROD:
                        before = k - NPROD
                        b = max(i for i in range(KD) if sum(TG[:i]) <= before)
                        act.wait_ge(pool_step, pool_steps(b, before - sum(TG[:b])))
                    act.activation(prod[:, k % NPROD, :], u[:, c % 2, t:t + S], ACT.Copy, scale=dw[:, c, t:t + 1]) \
                        .then_inc(prod_done, 1)
            hi(N_OUT + 1)
            for c in range(KD):
                square(2, c, v[:, c, :], vc_done, c + 1)
            table()
            root(2)
            for c in range(KD):
                act.wait_ge(t_done, KD * 2 + c + 1)
                act.activation(t_buf(c), t_buf(c), ACT.Silu, scale=vcol("ln_g", c),
                               bias=vcol("ln_b", c)).then_inc(yact_done, 1)
                act.wait_ge(yact_done, c + 1)
                act.activation(h_hi[:, c, :], t_buf(c), ACT.Copy).then_inc(hhi_done, 1)

            def out_steps(n0, m, nxt):
                for i in range(4):
                    if i < 2:
                        hi(n0 + i + 2)
                    elif i == 2:
                        hi(nxt)
                    for d in (2 * i, 2 * i + 1):
                        square(m, d, x[:, d, :], x_done, KD * (m - 2) + d + 1)
                hi(nxt + 1)

            table()
            out_steps(N_OUT, 3, N_UP[1])
            root(3)
            h_his(3, 0, 2)
            ffn(1, 4, N_UP[2])
            root(4)
            h_his(4, 1, 0)
            ffn(2, 5, N_QKV)
            root(5)
            h_his(5, 1, 1)

            def y_root(g):
                act.wait_ge(yv_done, g + 1)
                act.activation(y[:, 1, :], y[:, 0, :], ACT.Sqrt).then_inc(ysq_done, 1)

            for s in range(12):
                if s < 11:
                    hi(N_QKV + s + 2)
                if s < 8:
                    for c in (2 * s, 2 * s + 1):
                        act.wait_ge(qk_done, c + 1)
                        if c >= 2:
                            act.wait_ge(ind_done, c - 1)
                        act.activation(sq_tmp[:, c % 2, :], qk[:, c, :], ACT.Square).then_inc(qksq_done, 1)
                else:
                    act.wait_ge(slab_done, N_QKV + s + 1)
                    for b in range(2):
                        act.activation(v_hi[:, 2 * b:2 * b + 2, 256 * (s - 8):256 * (s - 7)],
                                       pair[s % 2][b].rearrange("p (c n) -> p c n", c=2), ACT.Copy) \
                            .then_inc(vhi_done, 1)
                if s == 4:
                    y_root(0)
                if s == 8:
                    y_root(1)

            def o_high(t):
                act.wait_ge(av_done, t + 1)
                q = slice(HD * (t % 2), HD * (t % 2) + HD)
                act.activation(h_hi[q, t // 2, :], ps[q, 6 + t % 2, :], ACT.Copy).then_inc(ohi_done, 1)

            def weights(t):
                for p in range(2):
                    act.wait_ge(cum_done, 2 * t + p + 1)
                    if t >= 1 and p == 0:
                        act.wait_ge(ahi_done, t)
                        act.wait_ge(alo_done, t)
                    act.activation(a_f[:, PIECE[p]], z_of(t, p), ACT.Exp).then_inc(a_done, 1)

            act.add_instruction(mybir.InstLoadActFuncSet(
                name=nc.get_next_instruction_name(), engine=mybir.EngineType.Activation, act_func_set_id=EXP_LN_SET))
            for t in range(HEADS):
                if t == 0:
                    act.wait_ge(bc_done, 2 * KD)
                for p in range(2):
                    w = sp_abs[:, t % 2, PIECE[p]]
                    act.wait_ge(z_done, 2 * t + p + 1)
                    if t >= 2:
                        act.wait_ge((splo_b_done, splo_a_done)[p], t - 1)
                    act.activation(w, z_of(t, p), ACT.Abs).then_inc(ln_step, 1)
                    act.wait_ge(ln_step, 6 * t + 3 * p + 1)
                    act.activation(w, w, ACT.Exp, scale=-1.0).then_inc(ln_step, 1)
                    act.wait_ge(ln_step, 6 * t + 3 * p + 2)
                    act.activation(w, w, ACT.Ln, bias=ones[:, 0:1]).then_inc(ln_step, 1)
                if t >= 1:
                    weights(t - 1)
                if t >= 2:
                    o_high(t - 2)
            weights(HEADS - 1)
            o_high(HEADS - 2)
            hi(N_WO + 1)
            o_high(HEADS - 1)
            table()
            out_steps(N_WO, 6, N_UP[3])
            root(6)
            h_his(6, 1, 2)
            ffn(3, None, None, last=True)

        @block.vector
        def _(dve):
            def lo(n, cols=SLAB):
                dve.wait_ge(hi_done, n + 1)
                dve.tensor_tensor(wsp[n % 2][:, 1, 0:cols], raw[n % 2][:, 0:cols], f32(wsp[n % 2][:, 0, 0:cols]), ALU.subtract) \
                    .then_inc(lo_done, 1)

            def ada_half(q, s, buf, acc, rows=4):
                for k in range(rows):
                    a = (sum(START_ROWS[:q]) if isinstance(q, int) and q < 6 else 8 * q + (STEP0 - 48)) + 4 * s + k
                    col = 4 * s + k
                    w = e_col[:, col:col + 1] if not isinstance(q, int) or q >= 2 else vcol("c", col)
                    if s == 0 and k == 0:
                        dve.tensor_scalar(acc, buf[:, k, :], w, None, ALU.mult).then_inc(ada_step, 1)
                    else:
                        dve.wait_ge(ada_step, a)
                        dve.scalar_tensor_tensor(out=acc, in0=buf[:, k, :], scalar=w, in1=acc, op0=ALU.mult,
                                                 op1=ALU.add).then_inc(ada_step, 1)

            def ada_take(q):
                dve.wait_ge(ada_sum, q + 1)
                if isinstance(q, int) and q < 2:
                    dst, b = e_pre[:, 4 * q:4 * q + 4], vcol("cond_b", 4 * q, 4)
                else:
                    dst = mods[:, :].rearrange("p (g n) -> p g n", n=4)[:, q - 2, :]
                    b = vcol("ada_b", 0, 144).rearrange("p (g n) -> p g n", n=4)[:, q - 2, :]
                dve.tensor_tensor(dst, ada_ps.rearrange("p (n b) -> p n b", b=2)[:, :, 0], b, ALU.add).then_inc(mod_done, 1)

            def factor(m):
                vv, sd, y0, y1 = st[:, 0:4], st[:, 4:8], st[:, 8:12], st[:, 16:20]
                dve.wait_ge(sqrt_done, m + 1)
                dve.tensor_scalar(vv, row[:, 0:4], 1.0 / D, EPS, ALU.mult, ALU.add).then_inc(vec_step, 1)
                dve.reciprocal(y0, sd).then_inc(vec_step, 1)
                dve.wait_ge(vec_step, 4 * m + 2)
                dve.tensor_tensor(y1, y0, y0, ALU.mult).then_inc(vec_step, 1)
                dve.wait_ge(vec_step, 4 * m + 3)
                dve.scalar_tensor_tensor(out=y1, in0=y1, scalar=-0.5, in1=vv, op0=ALU.mult, op1=ALU.mult) \
                    .then_inc(vec_step, 1)
                dve.wait_ge(vec_step, 4 * m + 4)
                dve.scalar_tensor_tensor(out=sd, in0=y1, scalar=1.5, in1=y0, op0=ALU.add, op1=ALU.mult) \
                    .then_inc(fac_step, 1)
                dve.wait_ge(fac_step, m + 1)
                dve.tensor_copy(st_r[:, :], sd).then_inc(facr_step, 1)
                for part in range(2):
                    if part == 1:
                        dve.tensor_tensor(y0, sd, f32(st_r[:, :]), ALU.subtract).then_inc(facr_step, 1)
                    dve.wait_ge(facr_step, 2 * m + part + 1)
                    dve.tensor_tensor(
                        (fac_hi, fac_lo)[part].rearrange("p (c m) -> p c m", c=4),
                        ident[:, :].rearrange("p (c m) -> p c m", c=1).broadcast_to((P, 4, P)),
                        (f32(st_r[:, :]), y0)[part].rearrange("p (c m) -> p c m", m=1).broadcast_to((P, 4, P)),
                        ALU.mult).then_inc(rdiag_done, 1)

            def h_lows(m, layer, sub):
                dve.wait_ge(mod_done, 2 + 18 * layer + 6 * sub + 4)
                dve.scalar_tensor_tensor(out=gs[:, :], in0=mod(layer, sub, 1), scalar=1.0,
                                         in1=vcol("norm_g", (3 * layer + sub) * KD, KD), op0=ALU.add,
                                         op1=ALU.mult).then_inc(gs_done, 1)
                if m:
                    factor(m)
                dve.wait_ge(gs_done, (m if m < 2 else m - 1) + 1)
                dve.wait_ge(row_done, m + 1)
                for c in range(0, KD, 2):
                    for b in (c, c + 1):
                        if b >= 4 and b % 2:
                            dve.wait_ge(h_odd_done, h_odd_parts(m) + b // 2 - 1)
                        elif b >= 4:
                            dve.wait_ge(h_done, h_parts(m) + b // 2 - 1)
                        dve.scalar_tensor_tensor(out=t_buf(b), in0=x[:, b, :], scalar=gs[:, b:b + 1],
                                                 in1=row, op0=ALU.mult, op1=ALU.mult).then_inc(t_done, 1)
                    dve.wait_ge(hhi_done, KD * m + c + 1)
                    dve.scalar_tensor_tensor(out=h_lo[:, c, :], in0=t_buf(c), scalar=mod(layer, sub, 0, c, 1),
                                             in1=f32(h_hi[:, c, :]), op0=ALU.add, op1=ALU.subtract) \
                        .then_inc(h_done, 1)

            def gate(layer, sub, k, factor_):
                dve.wait_ge(mod_done, 2 + 18 * layer + 6 * sub + 6)
                dve.tensor_scalar(gt[:, :], mod(layer, sub, 2), 1.0, factor_, ALU.add, ALU.mult).then_inc(gate_done, 1)
                dve.wait_ge(gate_done, k)

            def x_add(d, src):
                dve.scalar_tensor_tensor(out=x[:, d, :], in0=src, scalar=gt[:, d:d + 1], in1=x[:, d, :],
                                         op0=ALU.mult, op1=ALU.add).then_inc(x_done, 1)

            def up_step(j, i, s, ada, split=True, take=True):
                n = N_UP[j] + 2 * i + s
                f = KF * j + 2 * i + s
                dve.wait_ge(silu_done, f + 1)
                dve.tensor_tensor(act_tmp[:, s, :], act_tmp[:, s, :], pair[s][1], ALU.mult).then_inc(g_full, 1)
                dve.wait_ge(ghi_done, f + 1)
                dve.tensor_tensor(g_lo[:, 2 * i + s, :], act_tmp[:, s, :], f32(g_hi[:, 2 * i + s, :]),
                                  ALU.subtract).then_inc(g_done, 1)
                if split:
                    dve.wait_ge(hi_done, n + 3)
                    dve.tensor_tensor(wsp[s][:, 1, :], raw[s][:, :], f32(wsp[s][:, 0, :]), ALU.subtract) \
                        .then_inc(lo_done, 1)
                else:
                    lo(N_DOWN[j] + s, DOWN)
                if ada:
                    q = Q_FFN[j] + i
                    if s == 0 and take:
                        ada_take(q - 1)
                    dve.wait_ge(ada_s, 16 * (2 * q - 11 + s))
                    ada_half(q, s, ada_raw, ada_acc[:, :])

            def ffn(j, k, layer, sub, nxt, last=False):
                nb = Q_BODIES[j]
                if nb:
                    for s in range(2):
                        up_step(j, 0, s, True, take=False)
                    with dve.Fori(1, min(nb, 10)) as i:
                        for s in range(2):
                            up_step(j, i, s, True)
                if nb < 10:
                    with dve.Fori(nb, 10) as i:
                        for s in range(2):
                            up_step(j, i, s, False)
                    if nb:
                        ada_take(Q_FFN[j] + nb - 1)
                for s in range(2):
                    up_step(j, 10, s, nb == 11, split=False)
                gate(layer, sub, k, 0.5)
                for d in range(KD):
                    if d < KD - 1:
                        lo(N_DOWN[j] + 2 * d + 2, DOWN)
                    elif not last:
                        lo(nxt)
                    dve.wait_ge(slab_done, N_DOWN[j] + 2 * d + 2)
                    x_add(d, down_ps[d % 2])
                    if d < KD - 1:
                        lo(N_DOWN[j] + 2 * d + 3, DOWN)
                    if j == 0 and 1 <= d <= 6:
                        q, s = Q_DOWN + (d - 1) // 2, (d - 1) % 2
                        if s == 0:
                            ada_take(q - 1)
                        dve.wait_ge(ada_s, 16 * (2 * q - 11 + s))
                        ada_half(q, s, ada_raw, ada_acc[:, :])
                if nb == 11:
                    ada_take(Q_FFN[j] + 10 if j else Q_DOWN + 2)

            dve.wait_ge(ones_done, 2)
            dve.tensor_copy(ones_r[:, :], ones[:, :]).then_inc(ones_done, 1)
            dve.wait_ge(vec_s, 32)
            for q in range(6):
                if q == 2:
                    ada_take(1)
                    dve.wait_ge(e_done, 1)
                dve.wait_ge(stage_s[2 * q % 6], 16 * (q // 3 + 1))
                ada_half(q, 0, stage[2 * q % 6], act_tmp[:, q % 2, :])
                if q == 5:
                    factor(0)
                if q >= 1 and q != 2:
                    ada_take(q - 1)
                dve.wait_ge(stage_s[(2 * q + 1) % 6], 16 * (q // 3 + 1))
                ada_half(q, 1, stage[(2 * q + 1) % 6], act_tmp[:, q % 2, :], rows=START_ROWS[q] - 4)
            lo(N_UP[0])
            ada_take(5)
            h_lows(0, 0, 0)
            lo(N_UP[0] + 1)
            ffn(0, 1, 0, 0, N_CONV)
            h_lows(1, 0, 1)
            lo(N_CONV + 1)

            dve.wait_ge(dw_s, 16)
            dve.tensor_copy(dw_hi[:, :, :], dw[:, :, :]).then_inc(dws_done, 1)
            dve.wait_ge(dws_done, 1)
            dve.tensor_tensor(dw_lo[:, :, :], dw[:, :, :], f32(dw_hi[:, :, :]), ALU.subtract).then_inc(dws_done, 1)
            for b in range(2):
                dve.memset(u[:, b, 0:W - 1], 0.0)
                dve.memset(f32(u_hi[:, b, 0:W - 1]), 0.0)
                last = dve.memset(f32(u_lo[:, b, 0:W - 1]), 0.0)
                last.then_inc(pad_done, 1)
            dve.drain().then_inc(pad_done, 1)
            dve.wait_ge(pad_done, 3)

            def taps(c, lo_t, hi_t):
                before = sum(TV[:c])
                for t in range(lo_t, hi_t):
                    src = u[:, c % 2, t:t + S]
                    w = dw[:, c, t:t + 1]
                    dst = v[:, c, :] if t % 2 == 0 else v_odd[:, :]
                    if t == 0:
                        ins = dve.tensor_scalar(dst, src, w, vcol("dw_b", c), ALU.mult, ALU.add)
                    elif t == 1:
                        if c >= 1:
                            dve.wait_ge(vodd_done, c)
                        ins = dve.tensor_scalar(dst, src, w, None, ALU.mult)
                    else:
                        dve.wait_ge(tap_step, before + t - 1)
                        ins = dve.scalar_tensor_tensor(out=dst, in0=src, scalar=w, in1=dst, op0=ALU.mult, op1=ALU.add)
                    ins.then_inc(tap_step, 1)

            def combine(c):
                dve.wait_ge(tapp_done, c + 1)
                dve.wait_ge(vodd_done, c + 1)
                dve.tensor_tensor(v[:, c, :], v[:, c, :], down_ps[c % 2], ALU.add).then_inc(comb_step, 1)
                dve.wait_ge(comb_step, c + 1)
                dve.wait_ge(pool_step, pool_steps(c, TG[c] - 1))
                dve.tensor_tensor(v[:, c, :], v[:, c, :], v_pool[:, c % 2, :], ALU.add).then_inc(v_done, 1)

            for c in range(KD):
                dve.wait_ge(sig_done, c + 1)
                dve.scalar_tensor_tensor(out=u[:, c % 2, W - 1:], in0=pair[c % 2][0], scalar=vcol("b_in", c),
                                         in1=act_tmp[:, c % 2, :], op0=ALU.add, op1=ALU.mult).then_inc(u_done, 1)
                dve.wait_ge(uhi_done, c + 1)
                dve.tensor_tensor(u_lo[:, c % 2, W - 1:], u[:, c % 2, W - 1:], f32(u_hi[:, c % 2, W - 1:]),
                                  ALU.subtract).then_inc(ulo_done, 1)
                taps(c, 0, 4)
                if c < KD - 1:
                    lo(N_CONV + c + 2)
                taps(c, 4, 6)
                if 1 <= c < KD - 1:
                    combine(c - 1)
                taps(c, 6, TV[c])
                dve.wait_ge(tap_step, sum(TV[:c + 1]))
                dve.tensor_tensor(v[:, c, :], v[:, c, :], v_odd[:, :], ALU.add).then_inc(vodd_done, 1)
            combine(KD - 2)
            combine(KD - 1)
            dve.wait_ge(mean_done, 1)
            for c in range(KD):
                dve.scalar_tensor_tensor(out=v[:, c, :], in0=mean_row, scalar=-1.0 / D, in1=v[:, c, :], op0=ALU.mult,
                                         op1=ALU.add).then_inc(vc_done, 1)
            dve.wait_ge(sq_done, KD * 2 + 6)
            dve.tensor_tensor(prod[:, 4, :], prod[:, 4, :], prod[:, 5, :], ALU.add).then_inc(lns_step, 1)
            dve.wait_ge(sq_done, KD * 2 + 8)
            dve.tensor_tensor(prod[:, 6, :], prod[:, 6, :], prod[:, 7, :], ALU.add).then_inc(lns_step, 1)
            dve.wait_ge(lns_step, 2)
            dve.tensor_tensor(prod[:, 4, :], prod[:, 4, :], prod[:, 6, :], ALU.add).then_inc(lns_step, 1)
            dve.wait_ge(lns_step, 3)
            dve.wait_ge(ss_step, ss_steps(2) + 3)
            dve.tensor_tensor(prod[:, 4, :], prod[:, 4, :], ss[:, :], ALU.add).then_inc(lns_step, 1)
            lo(N_OUT + 1)
            factor(2)
            dve.wait_ge(row_done, 3)
            for c in range(KD + 1):
                if c < KD:
                    if c >= 4:
                        dve.wait_ge(h_done, h_parts(2) + c - 3)
                    dve.tensor_tensor(t_buf(c), v[:, c, :], row, ALU.mult).then_inc(t_done, 1)
                if c >= 1:
                    b = c - 1
                    dve.wait_ge(hhi_done, KD * 2 + b + 1)
                    dve.tensor_tensor(h_lo[:, b, :], t_buf(b), f32(h_hi[:, b, :]), ALU.subtract) \
                        .then_inc(h_done, 1)
            gate(0, 1, 2, 1.0)
            dve.tensor_tensor(gb[:, :], gt[:, :], vcol("b_out", 0, KD), ALU.mult).then_inc(gb_done, 1)
            dve.wait_ge(gb_done, 1)
            for d in range(KD):
                dve.tensor_scalar(x[:, d, :], x[:, d, :], gb[:, d:d + 1], None, ALU.add).then_inc(bo_step, 1)
            dve.wait_ge(bo_step, KD)
            for i in range(4):
                if i < 2:
                    lo(N_OUT + i + 2)
                elif i == 2:
                    lo(N_UP[1])
                for b in range(2):
                    if b == 0 and i >= 1:
                        dve.wait_ge(half_done, i)
                    else:
                        dve.wait_ge(slab_done, N_OUT + i + 1)
                    x_add(2 * i + b, pair[i % 2][b])
            h_lows(3, 0, 2)
            lo(N_UP[1] + 1)
            ffn(1, 3, 0, 2, N_UP[2])
            h_lows(4, 1, 0)
            lo(N_UP[2] + 1)
            ffn(2, 4, 1, 0, N_QKV)
            h_lows(5, 1, 1)
            lo(N_QKV + 1)

            dve.wait_ge(con_s, 48)
            dve.tensor_copy(con[:, :, :], con_f[:, :, :]).then_inc(conr_done, 1)
            dve.tensor_copy(sel[:, :, :], sel_f[:, :, :]).then_inc(conr_done, 1)

            def head_factors(g):
                dve.wait_ge(ind_done, KD * (g + 1))
                dve.tensor_scalar(y[:, 0, :], ps[0:32, 6 + g, :], 1.0 / HD, EPS, ALU.mult, ALU.add).then_inc(yv_done, 1)
                dve.wait_ge(ysq_done, g + 1)
                dve.reciprocal(y[:, 2, :], y[:, 1, :]).then_inc(yn_step, 1)
                dve.wait_ge(yn_step, 4 * g + 1)
                dve.tensor_tensor(y[:, 3, :], y[:, 2, :], y[:, 2, :], ALU.mult).then_inc(yn_step, 1)
                dve.wait_ge(yn_step, 4 * g + 2)
                dve.scalar_tensor_tensor(out=y[:, 3, :], in0=y[:, 3, :], scalar=-0.5, in1=y[:, 0, :], op0=ALU.mult,
                                         op1=ALU.mult).then_inc(yn_step, 1)
                dve.wait_ge(yn_step, 4 * g + 3)
                dve.scalar_tensor_tensor(out=y[:, 3, :], in0=y[:, 3, :], scalar=1.5, in1=y[:, 2, :], op0=ALU.add,
                                         op1=ALU.mult).then_inc(yn_step, 1)
                dve.wait_ge(yn_step, 4 * g + 4)
                if g == 1:
                    dve.wait_ge(bc_done, KD)
                dve.tensor_copy(y_hi[:, :], y[:, 3, :]).then_inc(y_done, 1)
                dve.wait_ge(y_done, 2 * g + 1)
                dve.tensor_tensor(y_lo[:, :], y[:, 3, :], f32(y_hi[:, :]), ALU.subtract).then_inc(y_done, 1)

            def normalise(b):
                dve.wait_ge(bc_done, b + 1)
                dve.scalar_tensor_tensor(out=qk[:, b, :], in0=qk[:, b, :], scalar=vcol("qk_g", b // KD),
                                         in1=spread_bank(b), op0=ALU.mult, op1=ALU.mult).then_inc(qkn_done, 1)

            for s in range(12):
                n = N_QKV + s
                dve.wait_ge(slab_done, n + 1)
                if s < 8:
                    for b in range(2):
                        dve.tensor_copy(qk[:, 2 * s + b, :], pair[s % 2][b]).then_inc(qk_done, 1)
                else:
                    for b in range(2):
                        dve.wait_ge(vhi_done, 2 * (s - 8) + b + 1)
                        at = (slice(None), slice(2 * b, 2 * b + 2), slice(256 * (s - 8), 256 * (s - 7)))
                        dve.tensor_tensor(v_lo[at], pair[s % 2][b].rearrange("p (c n) -> p c n", c=2),
                                          f32(v_hi[at]), ALU.subtract).then_inc(vlo_done, 1)
                if s < 11:
                    lo(n + 2)
                if s == 4:
                    head_factors(0)
                if s == 8:
                    head_factors(1)
                if s >= 5:
                    for b in range(2 * (s - 5), 2 * (s - 5) + 2):
                        normalise(b)

            def split_qk(c):
                b = c % 2
                if c >= 2:
                    dve.wait_ge(z_done, 4 * c - 4)
                if c <= 1:
                    dve.wait_ge(qkn_done, (KD + 1, 2 * KD)[c])
                dve.tensor_scalar(qk_s[:, b, 0, :], qk[:, c, :], HD ** -0.5, None, ALU.mult).then_inc(qks_step, 1)
                dve.tensor_copy(qk_s[:, b, 2, :], qk[:, KD + c, :]).then_inc(qks_step, 1)
                dve.wait_ge(qks_step, 4 * c + 1)
                dve.scalar_tensor_tensor(out=qk_s[:, b, 1, :], in0=qk[:, c, :], scalar=HD ** -0.5,
                                         in1=f32(qk_s[:, b, 0, :]), op0=ALU.mult, op1=ALU.subtract) \
                    .then_inc(qks_step, 1)
                dve.wait_ge(qks_step, 4 * c + 2)
                dve.tensor_tensor(qk_s[:, b, 3, :], qk[:, KD + c, :], f32(qk_s[:, b, 2, :]), ALU.subtract) \
                    .then_inc(qks_step, 1)

            def softplus(t, p):
                w = sp_abs[:, t % 2, PIECE[p]]
                dve.wait_ge(ln_step, 6 * t + 3 * p + 3)
                dve.scalar_tensor_tensor(out=w, in0=z_of(t, p), scalar=0.0, in1=w, op0=ALU.max, op1=ALU.add) \
                    .then_inc(sp_done, 1)
                dve.wait_ge(sp_done, 2 * t + p + 1)
                if t >= 1:
                    dve.wait_ge(cum_done, 2 * t)
                dve.tensor_copy(sp_hi[:, PIECE[p]], w).then_inc(sphi_done, 1)
                if p == 1:
                    dve.wait_ge(sphi_done, 2 * t + 2)
                    dve.tensor_tensor(sp_lo[:, PIECE[1]], w, f32(sp_hi[:, PIECE[1]]), ALU.subtract) \
                        .then_inc(splo_a_done, 1)

            def a_high(t):
                dve.wait_ge(a_done, 2 * t + 2)
                if t >= 1:
                    dve.wait_ge(av_done, t)
                dve.tensor_copy(a_hi[:, :], a_f[:, :]).then_inc(ahi_done, 1)

            def o_low(t):
                q = slice(HD * (t % 2), HD * (t % 2) + HD)
                dve.wait_ge(ohi_done, t + 1)
                dve.tensor_tensor(h_lo[q, t // 2, :], ps[q, 6 + t % 2, :], f32(h_hi[q, t // 2, :]), ALU.subtract) \
                    .then_inc(o_done, 1)

            split_qk(0)
            normalise(14)
            normalise(15)
            for t in range(HEADS):
                softplus(t, 0)
                softplus(t, 1)
                if t >= 1:
                    a_high(t - 1)
                if t >= 2:
                    o_low(t - 2)
                if t % 2 == 0 and t // 2 + 1 < KD:
                    split_qk(t // 2 + 1)
            a_high(HEADS - 1)
            o_low(HEADS - 2)
            lo(N_WO + 1)
            o_low(HEADS - 1)
            gate(1, 1, 5, 1.0)
            for i in range(4):
                if i < 2:
                    lo(N_WO + i + 2)
                elif i == 2:
                    lo(N_UP[3])
                for b in range(2):
                    if b == 0 and i >= 1:
                        dve.wait_ge(half_done, 3 + i)
                    else:
                        dve.wait_ge(slab_done, N_WO + i + 1)
                    x_add(2 * i + b, pair[i % 2][b])
            h_lows(6, 1, 2)
            lo(N_UP[3] + 1)
            ffn(3, 6, 1, 2, None, last=True)

        @block.tensor
        def _(pe):
            def triple(dst, a_hi_, a_lo_, b_hi_, b_lo_, start, stop):
                pe.matmul(dst, a_hi_, b_hi_, start=start, stop=False, skip_group_check=True)
                pe.matmul(dst, a_hi_, b_lo_, start=False, stop=False, skip_group_check=True)
                return pe.matmul(dst, a_lo_, b_hi_, start=False, stop=stop, skip_group_check=True)

            def two_chunks(slot, banks, m=None, between=None):
                w = wsp[slot]
                for k in range(KD):
                    if k == 2 and between:
                        between()
                    at = [slice((2 * k + b) * P, (2 * k + b + 1) * P) for b in range(2)]
                    if m is None:
                        for b in range(2):
                            last = triple(banks[b], w[:, 0, at[b]], w[:, 1, at[b]], h_hi[:, k, :], h_lo[:, k, :],
                                          k == 0, k == KD - 1)
                        continue
                    pe.wait_ge(hhi_done, KD * m + k + 1)
                    for b in range(2):
                        for part in range(2):
                            pe.matmul(banks[b], w[:, part, at[b]], h_hi[:, k, :], start=(k == 0 and part == 0),
                                      stop=False, skip_group_check=True)
                    if m == 2 or k % 2 == 0:
                        pe.wait_ge(h_done, h_parts(m) + (k if m == 2 else k // 2) + 1)
                    else:
                        pe.wait_ge(h_odd_done, h_odd_parts(m) + k // 2 + 1)
                    for b in range(2):
                        last = pe.matmul(banks[b], w[:, 0, at[b]], h_lo[:, k, :], start=False, stop=(k == KD - 1),
                                         skip_group_check=True)
                return last

            def two_chunks_in_turn(slot, banks):
                w = wsp[slot]
                for b in range(2):
                    for k in range(KD):
                        at = slice((2 * k + b) * P, (2 * k + b + 1) * P)
                        last = triple(banks[b], w[:, 0, at], w[:, 1, at], h_hi[:, k, :], h_lo[:, k, :],
                                      k == 0, k == KD - 1)
                    last.then_inc((half_done, slab_done)[b], 1)

            def stats(m):
                sums(m)
                spread(m)

            def sums(m):
                def add(src, first, sem_):
                    for c in range(4):
                        last = pe.matmul(row[:, c:c + 1], src[:, c * P:(c + 1) * P], ones[:, 0:1],
                                         start=(first and c == 0), stop=(not first or m == 2), skip_group_check=True)
                    if sem_ is not None:
                        last.then_inc(sem_, 1)

                if m == 2:
                    pe.wait_ge(lns_step, 4)
                    add(prod[:, 4, :], True, stat_done)
                else:
                    pe.wait_ge(ss_step, ss_steps(m) + 6)
                    add(ss, True, None)
                    pe.wait_ge(sq_done, KD * m + KD)
                    add(sq_tmp[:, 1, :], False, stat_done)

            def spread(m):
                pe.wait_ge(rdiag_done, 2 * m + 1)
                pe.matmul(row, ones_r[:, :], fac_hi, start=True, stop=False)
                pe.wait_ge(rdiag_done, 2 * m + 2)
                pe.matmul(row, ones_r[:, :], fac_lo, start=False, stop=True).then_inc(row_done, 1)

            def ada_reduce(q, acc):
                pe.wait_ge(ada_step, 8 * q + (STEP0 - 40))
                for c in range(4):
                    last = pe.matmul(ada_ps[:, 2 * c:2 * c + 1], acc[:, c * P:(c + 1) * P], ones[:, 0:1], start=True, stop=True)
                last.then_inc(ada_sum, 1)

            def ada_reduce_split(n):
                pe.wait_ge(accl_done, n)
                for c in range(4):
                    at = slice(c * P, (c + 1) * P)
                    pe.matmul(ada_ps[:, 2 * c:2 * c + 2], acc_hi[:, at], ones_r[:, 0:2], start=True, stop=False)
                    last = pe.matmul(ada_ps[:, 2 * c:2 * c + 2], acc_lo[:, at], ones_r[:, 0:2], start=False, stop=True)
                last.then_inc(ada_sum, 1)

            def start_group(q, between=None):
                if q == 2:
                    pe.wait_ge(e_done, 1)
                pe.wait_ge(stage_s[(2 * q + 1) % 6], 16 * (q // 3 + 1))
                if q >= 1:
                    pe.wait_ge(mod_done, q)
                w = stage[(2 * q + 1) % 6]
                for c in range(4):
                    for k in range(START_ROWS[q] - 4, 4):
                        b = e_col[:, 4 + k:5 + k] if q >= 2 else vcol("c", 4 + k)
                        last = pe.matmul(ada_ps[:, 2 * c:2 * c + 1], w[:, k, c * P:(c + 1) * P], b,
                                         start=(c == 0 and k == START_ROWS[q] - 4), stop=False, skip_group_check=True)
                last.then_inc(start_pe, 1)
                if between:
                    between()
                pe.wait_ge(ada_step, sum(START_ROWS[:q + 1]))
                for c in range(4):
                    last = pe.matmul(ada_ps[:, 2 * c:2 * c + 1], act_tmp[:, q % 2, c * P:(c + 1) * P], ones[:, 0:1],
                                     start=False, stop=True, skip_group_check=True)
                last.then_inc(ada_sum, 1)

            def up_step(j, i, s, m, ada):
                pe.wait_ge(lo_done, N_UP[j] + 2 * i + s + 1)
                reduce_ = (lambda: ada_reduce_split(N_SPLIT[j] + i)) if ada and s == 1 else None
                two_chunks(s, pair[s], m, reduce_).then_inc(slab_done, 1)

            def ffn(j, m):
                nb = Q_BODIES[j]
                up_step(j, 0, 0, m, False)
                up_step(j, 0, 1, None, False)
                if nb:
                    with pe.Fori(1, min(nb + 1, 11)) as i:
                        for s in range(2):
                            up_step(j, i, s, None, True)
                if nb < 11:
                    with pe.Fori(nb + 1, 11) as i:
                        for s in range(2):
                            up_step(j, i, s, None, False)
                with pe.Fori(0, KD // 2) as i:
                    for s in range(2):
                        for half in range(2):
                            pe.wait_ge(lo_done, N_DOWN[j] + 4 * i + 2 * s + half + 1)
                            pe.wait_ge(g_done, KF * j + HF * (half + 1))
                            w = wsp[half]
                            for k in range(HF):
                                at = slice(k * P, (k + 1) * P)
                                f = HF * half + k
                                last = triple(down_ps[s], w[:, 0, at], w[:, 1, at], g_hi[:, f, :], g_lo[:, f, :],
                                              f == 0, f == KF - 1)
                            last.then_inc(slab_done, 1)
                    if j == 0:
                        ada_reduce(Q_DOWN - 1 + i, ada_acc)
                if j and nb == 11:
                    ada_reduce(Q_FFN[j] + 10, ada_acc)

            pe.wait_ge(ones_done, 3)
            pe.wait_ge(vec_s, 32)
            for q in range(4):
                start_group(q)
            sums(0)
            start_group(4)
            start_group(5, lambda: spread(0))
            ffn(0, 0)
            stats(1)

            def conv_in(c):
                pe.wait_ge(lo_done, N_CONV + c + 1)
                if c >= 2:
                    pe.wait_ge(u_done, c - 1)
                two_chunks(c % 2, pair[c % 2], 1 if c == 0 else None).then_inc(slab_done, 1)

            def conv_taps(c):
                pe.wait_ge(tapw_done, 2 * c + 2)
                pe.wait_ge(ulo_done, c + 1)
                if c >= 2:
                    pe.wait_ge(v_done, c - 1)
                w = taps_w[:, c % 2, :, :]
                for t in range(TP[c]):
                    at = slice(t * P, (t + 1) * P)
                    u0 = W - TP[c] + t
                    last = triple(down_ps[c % 2], w[:, 0, at], w[:, 1, at], u_hi[:, c % 2, u0:u0 + S],
                                  u_lo[:, c % 2, u0:u0 + S], t == 0, t == TP[c] - 1)
                last.then_inc(tapp_done, 1)

            for c in range(KD):
                conv_in(c)
                if c >= 1:
                    conv_taps(c - 1)
            conv_taps(KD - 1)
            pe.wait_ge(vsum_step, KD - 2)
            pe.matmul(mean_row, ones[:, :], v_sum[:, :], start=True, stop=False)
            pe.wait_ge(v_done, KD)
            pe.matmul(mean_row, ones[:, :], v[:, KD - 1, :], start=False, stop=True).then_inc(mean_done, 1)
            stats(2)
            for i in range(4):
                pe.wait_ge(lo_done, N_OUT + i + 1)
                if i >= 2:
                    pe.wait_ge(x_done, KD + 2 * (i - 1))
                if i == 0:
                    two_chunks(0, pair[0], 2).then_inc(slab_done, 1)
                else:
                    two_chunks_in_turn(i % 2, pair[i % 2])
            stats(3)
            ffn(1, 3)
            stats(4)
            ffn(2, 4)
            stats(5)

            def head_sums(c):
                pe.wait_ge(con_s, 48)
                pe.wait_ge(qksq_done, c + 1)
                pe.matmul(ps[0:32, 6 + c // KD, :], ind[:, c % KD, :], sq_tmp[:, c % 2, :], start=(c % KD == 0),
                          stop=(c % KD == KD - 1)).then_inc(ind_done, 1)

            def head_spread(b):
                pe.wait_ge(y_done, 2 * (b // KD) + 2)
                if 2 <= b < 14:
                    pe.wait_ge(qkn_done, b - 1)
                w = sel[:, b % KD, :]
                pe.matmul(spread_bank(b), w, y_hi[:, :], start=True, stop=False)
                pe.matmul(spread_bank(b), w, y_lo[:, :], start=False, stop=True).then_inc(bc_done, 1)

            for s in range(12):
                n = N_QKV + s
                pe.wait_ge(lo_done, n + 1)
                if s < 8:
                    two_chunks(s % 2, pair[s % 2], 5 if s == 0 else None).then_inc(slab_done, 1)
                else:
                    w = wsp[s % 2]
                    for c in range(4):
                        dst = pair[s % 2][c // 2][:, 256 * (c % 2):256 * (c % 2) + 256]
                        for k in range(KD):
                            at = slice(2 * P * k, 2 * P * (k + 1))
                            cols = slice(P * c, P * (c + 1))
                            last = triple(dst, h_hi[:, k, cols], h_lo[:, k, cols], w[:, 0, at], w[:, 1, at],
                                          k == 0, k == KD - 1)
                    last.then_inc(slab_done, 1)
                if 1 <= s <= 8:
                    head_sums(2 * s - 2)
                    head_sums(2 * s - 1)
                if s >= 5:
                    for b in range(2 * (s - 5), 2 * (s - 5) + 2):
                        head_spread(b)

            at_key = [0, S, 2 * S, 2 * S - P]

            def span(base, c, q0):
                return slice(base + at_key[c] + q0 - P * c, base + at_key[c] + S - P * c)

            def logits(t):
                base = 3 * S * (t % 2)
                c2, half = t // 2, t % 2
                rows = slice(HD * half, HD * half + HD)
                pe.wait_ge(qks_step, 4 * c2 + 4)
                if t == 1:
                    pe.wait_ge(qkn_done, 2 * KD)
                if t == 0:
                    pe.wait_ge(conr_done, 2)
                    pe.wait_ge(vlo_done, 8)
                for p, blocks in enumerate(((1, 3, 2), (0,))):
                    if t >= 2:
                        pe.wait_ge(a_done, 2 * (t - 2) + p + 1)
                    for c in blocks:
                        pe.matmul(zps[:, base + at_key[c]:base + at_key[c] + P], con[:, 0, :], con[:, 1, :],
                                  start=(c != 3), stop=False, skip_group_check=True)
                    for c in blocks:
                        keys = slice(P * c, P * (c + 1))
                        seen = slice(P * c, S)
                        last = triple(zps[:, span(base, c, P * c)], qk_s[rows, c2 % 2, 2, keys],
                                      qk_s[rows, c2 % 2, 3, keys], qk_s[rows, c2 % 2, 0, seen],
                                      qk_s[rows, c2 % 2, 1, seen], False, False)
                    last.then_inc(z_done, 1)

            def suffix(t):
                base = 3 * S * (t % 2)
                for p, blocks in enumerate(((1, 2, 3), (0,))):
                    for part in (sp_hi, sp_lo):
                        if part is sp_hi:
                            pe.wait_ge(sphi_done, 2 * t + p + 1)
                        else:
                            pe.wait_ge((splo_b_done, splo_a_done)[p], t + 1)
                        for c in blocks:
                            for later in range(c, 4):
                                last = pe.matmul(zps[:, span(base, c, P * later)],
                                                 con[:, 2 if later == c else 3, :],
                                                 part[:, span(0, later, P * later)],
                                                 start=False, stop=(part is sp_lo), skip_group_check=True)
                    last.then_inc(cum_done, 1)

            def values(t):
                c2 = t // 2
                cols = slice(P * c2, P * (c2 + 1))
                pe.wait_ge(ahi_done, t + 1)
                pe.wait_ge(alo_done, t + 1)
                if t >= 2:
                    pe.wait_ge(o_done, t - 1)
                for c in range(4):
                    last = triple(ps[:, 6 + t % 2, P * c:S], v_hi[:, c, cols], v_lo[:, c, cols],
                                  a_hi[:, span(0, c, P * c)], a_lo[:, span(0, c, P * c)], c == 0, c == 3)
                last.then_inc(av_done, 1)

            head_spread(14)
            head_spread(15)
            logits(0)
            for t in range(HEADS):
                if t + 1 < HEADS:
                    logits(t + 1)
                suffix(t)
                if t >= 1:
                    values(t - 1)
            pe.wait_ge(lo_done, N_WO + 1)
            pe.wait_ge(a_done, 2 * (HEADS - 1))
            for k in range(KD):
                if k == KD - 1:
                    values(HEADS - 1)
                pe.wait_ge(o_done, 2 * k + 2)
                for b in range(2):
                    at = slice((2 * k + b) * P, (2 * k + b + 1) * P)
                    last = triple(pair[0][b], wsp[0][:, 0, at], wsp[0][:, 1, at], h_hi[:, k, :], h_lo[:, k, :],
                                  k == 0, k == KD - 1)
            last.then_inc(slab_done, 1)
            for i in range(1, 4):
                pe.wait_ge(lo_done, N_WO + i + 1)
                if i >= 2:
                    pe.wait_ge(x_done, 4 * KD + 2 * (i - 1))
                two_chunks_in_turn(i % 2, pair[i % 2])
            stats(6)
            ffn(3, 6)


def kernel(**inputs):
    import concourse.bacc as bacc
    from concourse.bass_utils import run_bass_kernel_spmd

    a = {k: np.asarray(v) for k, v in inputs.items()}

    def cols(v):
        return np.ascontiguousarray(v.reshape(-1, P).T)

    def slabs(w, rows, width):
        w = w.reshape(-1, w.shape[-2] // (rows * P), rows, P, w.shape[-1] // width, width)
        return w.transpose(0, 4, 1, 3, 2, 5).reshape(-1, P, rows * width)

    up = np.stack([a["ffn_w1"].reshape(NFFN, KD, P, KF, P), a["ffn_w3"].reshape(NFFN, KD, P, KF, P)], axis=4)
    up = up.transpose(0, 3, 2, 1, 4, 5).reshape(NFFN * KF, P, SLAB)
    down = slabs(a["ffn_w2"].reshape(NFFN, F, D), HF, P)
    w_in = a["a_w_in"][0].reshape(KD, P, 2, KD, P).transpose(3, 1, 0, 2, 4).reshape(KD, P, SLAB)
    mix = np.concatenate([w_in, slabs(a["a_w_out"][0], KD, 2 * P), slabs(a["b_w_qkv"][0], KD, 2 * P),
                          slabs(a["b_w_o"][0], KD, 2 * P)])
    ada = np.concatenate([slabs(a["cond_w"], 4, GW), slabs(a["ada_w"][0], 4, GW), slabs(a["ada_w"][1], 4, GW)])
    head = lambda g: np.concatenate([g, g]).reshape(P, 1)
    vec = np.concatenate([
        cols(a["norm_g"]), cols(a["ada_b"]), cols(a["cond_b"]), cols(a["c"]), cols(a["a_b_in"][0]),
        cols(a["a_dw_b"][0]), cols(a["a_ln_g"][0]), cols(a["a_ln_b"][0]), cols(a["a_b_out"][0]),
        head(a["b_q_g"][0]), head(a["b_k_g"][0])], axis=1)
    dw = a["a_dw"][0].reshape(W, KD, P).transpose(2, 1, 0)
    x_t = a["x"][0].reshape(S, KD, P).transpose(2, 1, 0)
    i = np.arange(P)
    con = np.stack([np.eye(P), np.where(i[:, None] >= i[None, :], NEG, 0.0),
                    np.where(i[:, None] >= i[None, :], -1.0, 0.0), -np.ones((P, P))], axis=1)
    ind = np.zeros((P, KD, 32))
    sel = np.zeros((32, KD, P))
    for c in range(KD):
        for b in range(2):
            ind[HD * b:HD * (b + 1), c, 2 * c + b] = 1.0
            sel[2 * c + b, c, HD * b:HD * (b + 1)] = 1.0

    nc = bacc.Bacc("TRN2", target_bir_lowering=False, num_devices=1)
    arrays, args = {}, []
    for name, v in (("x_t", x_t), ("up", up), ("down", down), ("mix", mix), ("ada", ada), ("vec", vec), ("dw", dw),
                    ("con", con), ("ind", ind), ("sel", sel)):
        v = np.ascontiguousarray(v, dtype=np.float32)
        arrays[name + "_d"] = v
        args.append(nc.dram_tensor(name + "_d", v.shape, F32, kind="ExternalInput").ap())
    out = nc.dram_tensor("out_t", (P, KD, S), F32, kind="ExternalOutput").ap()
    trunk(nc, *args, out)
    r = run_bass_kernel_spmd(nc, [arrays], core_ids=[0])
    got = r.results[0]["out_t"]
    return np.ascontiguousarray(got.transpose(2, 1, 0).reshape(1, S, D))
```
